# Optimizing a Trainium2 kernel written in Bass

```python
import math
import jax, jax.numpy as jnp
from jax import lax
import numpy as np

D_MODEL = 1024
BATCH = 1
SEQ = 512
DEPTH = 1

N_META = 16
BLOCK = 128
WINDOW = 128
HEAD_DIM = 64
A_HEADS = D_MODEL // 256
A_V_DIM = 2 * HEAD_DIM
A_WIDTH = A_HEADS * A_V_DIM
B_HEADS = D_MODEL // 128
B_KV_HEADS = max(1, B_HEADS // 4)
B_GROUP = B_HEADS // B_KV_HEADS
B_WIDTH = B_HEADS * HEAD_DIM
D_FF = -(-8 * D_MODEL // (3 * 256)) * 256
EPS = 1e-6
QA_W = A_HEADS * 2 * HEAD_DIM
KA_W = A_HEADS * 2 * HEAD_DIM
VA_W = A_WIDTH
QB_W = B_WIDTH
KB_W = B_KV_HEADS * HEAD_DIM
VB_W = B_KV_HEADS * HEAD_DIM
GATE_W = D_MODEL
PROJ_W = QA_W + KA_W + VA_W + QB_W + KB_W + VB_W + 2 * GATE_W


def rms_norm(x, g):
    xf = x.astype(jnp.float32)
    y = xf * lax.rsqrt(jnp.mean(xf * xf, axis=-1, keepdims=True) + EPS)
    return (y * g.astype(jnp.float32)).astype(x.dtype)

def alibi_slopes(n):
    return jnp.asarray(2.0 ** (-8.0 * np.arange(1, n + 1) / n), dtype=jnp.float32)

def lambda_init_for(layer):
    return 0.8 - 0.6 * math.exp(-0.3 * layer)

def diff_attn_rows(q1, q2, k1, k2, v, qpos, kpos, key_real, slopes, lam):
    scale = HEAD_DIM ** -0.5
    dist = jnp.abs(qpos[:, None] - kpos[None, :]).astype(jnp.float32) * key_real[None, :]
    bias = -slopes[:, None, None] * dist[None]
    s1 = jnp.einsum('bqhd,bkhd->bhqk', q1, k1).astype(jnp.float32) * scale + bias
    s2 = jnp.einsum('bqhd,bkhd->bhqk', q2, k2).astype(jnp.float32) * scale + bias
    attn = jax.nn.softmax(s1, axis=-1) - lam * jax.nn.softmax(s2, axis=-1)
    return jnp.einsum('bhqk,bkhe->bqhe', attn.astype(v.dtype), v)

def differential_attention(q, k, v, lam_q1, lam_k1, lam_q2, lam_k2, subln_g, lambda_init):
    Bn, L = q.shape[0], q.shape[1]
    S = L - N_META
    nb = S // BLOCK
    pos = jnp.arange(L)
    key_real = (pos >= N_META).astype(jnp.float32)
    slopes = alibi_slopes(A_HEADS)
    lam = (jnp.exp(jnp.sum(lam_q1.astype(jnp.float32) * lam_k1.astype(jnp.float32)))
           - jnp.exp(jnp.sum(lam_q2.astype(jnp.float32) * lam_k2.astype(jnp.float32)))
           + lambda_init)
    q1, q2 = q[..., 0, :], q[..., 1, :]
    k1, k2 = k[..., 0, :], k[..., 1, :]

    def attend(a, b, p):
        return diff_attn_rows(a, b, k1, k2, v, p, pos, key_real, slopes, lam)

    y_meta = attend(q1[:, :N_META], q2[:, :N_META], pos[:N_META])

    def to_blocks(t):
        return t[:, N_META:].reshape(Bn, nb, BLOCK, *t.shape[2:]).swapaxes(0, 1)

    y_real = lax.map(lambda a: attend(*a),
                     (to_blocks(q1), to_blocks(q2), pos[N_META:].reshape(nb, BLOCK)))
    y_real = y_real.swapaxes(0, 1).reshape(Bn, S, A_HEADS, A_V_DIM)
    y = jnp.concatenate([y_meta, y_real], axis=1)
    y = rms_norm(y, subln_g) * (1.0 - lambda_init)
    return y.reshape(Bn, L, A_WIDTH)

def window_attn_blocks(q, k, v, qpos, kpos, kvalid, kreal, slopes, sink):
    scale = HEAD_DIM ** -0.5
    dt = jnp.abs(qpos[:, :, None] - kpos[:, None, :])
    visible = kvalid[:, None, :] & ((~kreal[:, None, :]) | (dt <= WINDOW))
    dist = jnp.where(kreal[:, None, :], dt, 0).astype(jnp.float32)
    bias = -slopes[None, :, :, None, None] * dist[:, None, None]
    s = jnp.einsum('bnqgrd,bnkgd->bngrqk', q, k).astype(jnp.float32) * scale + bias
    s = jnp.where(visible[None, :, None, None], s, -jnp.inf)
    sink_b = sink.astype(jnp.float32)[None, None, :, :, None, None]
    m = jnp.maximum(jnp.max(s, axis=-1, keepdims=True), sink_b)
    p = jnp.exp(s - m)
    denom = jnp.sum(p, axis=-1, keepdims=True) + jnp.exp(sink_b - m)
    return jnp.einsum('bngrqk,bnkgd->bnqgrd', (p / denom).astype(v.dtype), v)

def windowed_gqa(q, k, v, sink):
    Bn, L = q.shape[0], q.shape[1]
    S = L - N_META
    nb = S // BLOCK
    G, d = B_KV_HEADS, HEAD_DIM
    slopes = alibi_slopes(B_HEADS).reshape(B_KV_HEADS, B_GROUP)

    def band(t):
        tp = jnp.pad(t[:, N_META:], ((0, 0), (BLOCK, BLOCK), (0, 0), (0, 0)))
        tp = tp.reshape(Bn, nb + 2, BLOCK, G, d)
        win = jnp.concatenate([tp[:, j:j + nb] for j in range(3)], axis=2)
        meta = jnp.broadcast_to(t[:, None, :N_META], (Bn, nb, N_META, G, d))
        return jnp.concatenate([meta, win], axis=2)

    blk = jnp.arange(nb)[:, None]
    win_idx = (blk - 1) * BLOCK + jnp.arange(3 * BLOCK)[None, :]
    meta_pos = jnp.broadcast_to(jnp.arange(N_META)[None, :], (nb, N_META))
    kpos = jnp.concatenate([meta_pos, N_META + win_idx], axis=1)
    kvalid = jnp.concatenate([jnp.ones((nb, N_META), bool),
                              (win_idx >= 0) & (win_idx < S)], axis=1)
    kreal = jnp.concatenate([jnp.zeros((nb, N_META), bool),
                             jnp.ones((nb, 3 * BLOCK), bool)], axis=1)
    qpos = N_META + jnp.arange(S).reshape(nb, BLOCK)
    q_real = q[:, N_META:].reshape(Bn, nb, BLOCK, G, B_GROUP, d)
    y_real = window_attn_blocks(q_real, band(k), band(v), qpos, kpos, kvalid, kreal, slopes, sink)
    y_real = y_real.reshape(Bn, S, B_WIDTH)

    tk = N_META + BLOCK
    kpos_m = jnp.arange(tk)[None, :]
    y_meta = window_attn_blocks(q[:, None, :N_META], k[:, None, :tk], v[:, None, :tk],
                                jnp.arange(N_META)[None, :], kpos_m,
                                jnp.ones((1, tk), bool), kpos_m >= N_META, slopes, sink)
    y_meta = y_meta.reshape(Bn, N_META, B_WIDTH)
    return jnp.concatenate([y_meta, y_real], axis=1)

def mixer_block(h, w_in, lq1, lk1, lq2, lk2, subln_g, sink, w_ba, w_bb, w_o, lambda_init):
    Bn, L = h.shape[0], h.shape[1]
    proj = h @ w_in
    o = 0
    qa = proj[..., o:o + QA_W]; o += QA_W
    ka = proj[..., o:o + KA_W]; o += KA_W
    va = proj[..., o:o + VA_W]; o += VA_W
    qb = proj[..., o:o + QB_W]; o += QB_W
    kb = proj[..., o:o + KB_W]; o += KB_W
    vb = proj[..., o:o + VB_W]; o += VB_W
    ga = proj[..., o:o + GATE_W]; o += GATE_W
    gb = proj[..., o:o + GATE_W]
    y_a = differential_attention(qa.reshape(Bn, L, A_HEADS, 2, HEAD_DIM),
                                 ka.reshape(Bn, L, A_HEADS, 2, HEAD_DIM),
                                 va.reshape(Bn, L, A_HEADS, A_V_DIM),
                                 lq1, lk1, lq2, lk2, subln_g, lambda_init)
    y_b = windowed_gqa(qb.reshape(Bn, L, B_KV_HEADS, B_GROUP, HEAD_DIM),
                       kb.reshape(Bn, L, B_KV_HEADS, HEAD_DIM),
                       vb.reshape(Bn, L, B_KV_HEADS, HEAD_DIM),
                       sink.reshape(B_KV_HEADS, B_GROUP))
    merged = jax.nn.sigmoid(ga) * (y_a @ w_ba) + jax.nn.sigmoid(gb) * (y_b @ w_bb)
    return merged @ w_o

def swiglu(h, w_gate, w_up, w_down):
    return (jax.nn.silu(h @ w_gate) * (h @ w_up)) @ w_down

def first_inputs(seed: int = 0) -> dict:
    key = jax.random.key(seed)
    ks = jax.random.split(key, 20)

    def w(k, shape, fan_in):
        return jax.random.normal(k, shape, jnp.float32) * (fan_in ** -0.5)

    def gain(k, shape):
        return 1.0 + 0.02 * jax.random.normal(k, shape, jnp.float32)

    return {
        "x": jax.random.normal(ks[0], (BATCH, SEQ, D_MODEL), jnp.float32),
        "meta_tokens": jax.random.normal(ks[1], (N_META, D_MODEL), jnp.float32),
        "norm_mix": gain(ks[2], (DEPTH, D_MODEL)),
        "w_in": w(ks[3], (DEPTH, D_MODEL, PROJ_W), D_MODEL),
        "lambda_q1": 0.1 * jax.random.normal(ks[4], (DEPTH, HEAD_DIM), jnp.float32),
        "lambda_k1": 0.1 * jax.random.normal(ks[5], (DEPTH, HEAD_DIM), jnp.float32),
        "lambda_q2": 0.1 * jax.random.normal(ks[6], (DEPTH, HEAD_DIM), jnp.float32),
        "lambda_k2": 0.1 * jax.random.normal(ks[7], (DEPTH, HEAD_DIM), jnp.float32),
        "subln_gain": gain(ks[8], (DEPTH, A_V_DIM)),
        "sink_logits": 0.5 * jax.random.normal(ks[9], (DEPTH, B_HEADS), jnp.float32),
        "w_branch_a": w(ks[10], (DEPTH, A_WIDTH, D_MODEL), A_WIDTH),
        "w_branch_b": w(ks[11], (DEPTH, B_WIDTH, D_MODEL), B_WIDTH),
        "w_out": w(ks[12], (DEPTH, D_MODEL, D_MODEL), D_MODEL),
        "norm_ffn": gain(ks[13], (DEPTH, D_MODEL)),
        "w_ff_gate": w(ks[14], (DEPTH, D_MODEL, D_FF), D_MODEL),
        "w_ff_up": w(ks[15], (DEPTH, D_MODEL, D_FF), D_MODEL),
        "w_ff_down": w(ks[16], (DEPTH, D_FF, D_MODEL), D_FF),
        "norm_final": gain(ks[17], (D_MODEL,)),
    }

def first_block(x, meta_tokens, norm_mix, w_in, lambda_q1, lambda_k1, lambda_q2, lambda_k2,
              subln_gain, sink_logits, w_branch_a, w_branch_b, w_out, norm_ffn,
              w_ff_gate, w_ff_up, w_ff_down, norm_final):
    Bn = x.shape[0]
    meta = jnp.broadcast_to(meta_tokens.astype(x.dtype)[None], (Bn, N_META, x.shape[-1]))
    h = jnp.concatenate([meta, x], axis=1)
    for layer in range(DEPTH):
        h = h + mixer_block(rms_norm(h, norm_mix[layer]), w_in[layer],
                            lambda_q1[layer], lambda_k1[layer], lambda_q2[layer], lambda_k2[layer],
                            subln_gain[layer], sink_logits[layer],
                            w_branch_a[layer], w_branch_b[layer], w_out[layer],
                            lambda_init_for(layer))
        h = h + swiglu(rms_norm(h, norm_ffn[layer]), w_ff_gate[layer], w_ff_up[layer], w_ff_down[layer])
    return rms_norm(h, norm_final)[:, N_META:]


DEPTH_2 = 2

N_A_LAYERS = (DEPTH_2 + 1) // 2
N_C_LAYERS = DEPTH_2 // 2
D_FF_2 = 4 * D_MODEL
NEG = -1e30

CONV_WIDTH = D_MODEL // 2
CONV_GROUPS = 8
CONV_K = 3
MLA_HEADS = 8
MLA_NOPE = 64
MLA_ROPE = 32
MLA_V = 64
MLA_KV_RANK = 256
MLA_Q_RANK = 3 * MLA_KV_RANK
ROPE_THETA = 10000.0
MLA_Q_BLOCK = 128
A_IN = 3 * CONV_WIDTH + MLA_Q_RANK + MLA_KV_RANK + MLA_ROPE
A_MIX = CONV_WIDTH + MLA_HEADS * MLA_V
NSA_HEADS = 16
NSA_GROUPS = 4
NSA_REP = NSA_HEADS // NSA_GROUPS
NSA_DH = 64
CMP_LEN = 32
CMP_STRIDE = 16
SLC_LEN = 64
N_SEL = 16
WINDOW_2 = 512
NSA_Q_BLOCK = 32
FORCE_BONUS = 1e4
KV_W = NSA_GROUPS * NSA_DH
C_MIX = NSA_HEADS * NSA_DH
C_IN = C_MIX + 6 * KV_W + 3 * NSA_HEADS


def rms_norm_2(x, g):
    xf = x.astype(jnp.float32)
    y = xf * lax.rsqrt(jnp.mean(xf * xf, axis=-1, keepdims=True) + EPS)
    return (y * g.astype(jnp.float32)).astype(x.dtype)

def alibi_slopes_2(n):
    return jnp.asarray(2.0 ** (-8.0 * np.arange(1, n + 1) / n), jnp.float32)

def rope(x, pos):
    half = x.shape[-1] // 2
    inv = ROPE_THETA ** (-jnp.arange(half, dtype=jnp.float32) / half)
    ang = pos.astype(jnp.float32)[:, None] * inv[None, :]
    cos, sin = jnp.cos(ang)[:, None, :], jnp.sin(ang)[:, None, :]
    x1 = x[..., :half].astype(jnp.float32)
    x2 = x[..., half:].astype(jnp.float32)
    return jnp.concatenate([x1 * cos - x2 * sin, x2 * cos + x1 * sin], axis=-1).astype(x.dtype)

def short_conv(u, w):
    c = u.shape[-1]
    return lax.conv_general_dilated(u, w[:, None, :].astype(u.dtype), window_strides=(1,),
                                    padding=[(CONV_K - 1, 0)],
                                    dimension_numbers=('NWC', 'WIO', 'NWC'),
                                    feature_group_count=c)

def dense_causal_attention(q, k, v):
    b, s, h, d = q.shape
    nb = s // MLA_Q_BLOCK
    scale = d ** -0.5
    qb = q.reshape(b, nb, MLA_Q_BLOCK, h, d).transpose(1, 0, 2, 3, 4)
    kpos = jnp.arange(s)

    def one(args):
        q_blk, i = args
        t = i * MLA_Q_BLOCK + jnp.arange(MLA_Q_BLOCK)
        sc = jnp.einsum('bqhd,bshd->bhqs', q_blk, k).astype(jnp.float32) * scale
        sc = jnp.where(kpos[None, :] <= t[:, None], sc, NEG)
        p = jax.nn.softmax(sc, axis=-1).astype(v.dtype)
        return jnp.einsum('bhqs,bshd->bqhd', p, v)

    out = lax.map(one, (qb, jnp.arange(nb)))
    return out.transpose(1, 0, 2, 3, 4).reshape(b, s, h, v.shape[-1])

def mixer_a(xn, w_in, conv_w, q_norm, w_q_up, kv_norm, w_kv_up, w_out):
    b, s, _ = xn.shape
    proj = xn @ w_in
    o1 = CONV_WIDTH; o2 = 2 * CONV_WIDTH; o3 = 3 * CONV_WIDTH
    o4 = o3 + MLA_Q_RANK; o5 = o4 + MLA_KV_RANK
    g_b, g_c, hv, c_q, c_kv, k_r = jnp.split(proj, [o1, o2, o3, o4, o5], axis=-1)
    y_conv = g_b * short_conv(g_c * hv, conv_w)
    pos = jnp.arange(s)
    q = (rms_norm_2(c_q, q_norm) @ w_q_up).reshape(b, s, MLA_HEADS, MLA_NOPE + MLA_ROPE)
    q = jnp.concatenate([q[..., :MLA_NOPE], rope(q[..., MLA_NOPE:], pos)], axis=-1)
    kv = (rms_norm_2(c_kv, kv_norm) @ w_kv_up).reshape(b, s, MLA_HEADS, MLA_NOPE + MLA_V)
    k_rope = jnp.broadcast_to(rope(k_r[:, :, None, :], pos), (b, s, MLA_HEADS, MLA_ROPE))
    k = jnp.concatenate([kv[..., :MLA_NOPE], k_rope], axis=-1)
    v = kv[..., MLA_NOPE:]
    y_mla = dense_causal_attention(q, k, v).reshape(b, s, MLA_HEADS * MLA_V)
    return jnp.concatenate([y_conv, y_mla], axis=-1) @ w_out

def mixer_c(xn, w_in, pe_k, w1_k, w2_k, pe_v, w1_v, w2_v, w_out):
    b, s, _ = xn.shape
    G, R, Dh, QB = NSA_GROUPS, NSA_REP, NSA_DH, NSA_Q_BLOCK
    proj = xn @ w_in
    q = proj[..., :C_MIX].reshape(b, s, G, R, Dh)
    kvs = jnp.moveaxis(proj[..., C_MIX:C_MIX + 6 * KV_W].reshape(b, s, 6, G, Dh), 2, 0)
    k_c, v_c, k_s, v_s, k_w, v_w = kvs
    gates = jax.nn.sigmoid(proj[..., C_MIX + 6 * KV_W:].astype(jnp.float32))
    gates = gates.reshape(b, s, 3, G, R).astype(xn.dtype)

    n_cmp = (s - CMP_LEN) // CMP_STRIDE + 1
    starts = np.arange(n_cmp) * CMP_STRIDE
    idx = starts[:, None] + np.arange(CMP_LEN)[None, :]

    def compress(z, pe, w1, w2):
        blk = z[:, idx] + pe[:, None, :]
        hdn = jax.nn.gelu(jnp.einsum('bnlgd,lde->bnge', blk, w1))
        return hdn @ w2

    kc = compress(k_c, pe_k, w1_k, w2_k)
    vc = compress(v_c, pe_v, w1_v, w2_v)
    cmp_centre = jnp.asarray(starts + (CMP_LEN - 1) / 2.0, jnp.float32)
    cmp_end = jnp.asarray(starts + CMP_LEN - 1, jnp.int32)

    n_slc = s // SLC_LEN
    n_sel = min(N_SEL, n_slc)
    ss = np.arange(n_slc) * SLC_LEN
    ov = np.clip(np.minimum(starts[:, None] + CMP_LEN, ss[None, :] + SLC_LEN)
                 - np.maximum(starts[:, None], ss[None, :]), 0, None) / CMP_LEN
    ov = jnp.asarray(ov, jnp.float32)
    kb = k_s.reshape(b, n_slc, SLC_LEN, G, Dh).transpose(0, 3, 1, 2, 4)
    vb = v_s.reshape(b, n_slc, SLC_LEN, G, Dh).transpose(0, 3, 1, 2, 4)

    kwp = jnp.pad(k_w, ((0, 0), (WINDOW_2, 0), (0, 0), (0, 0)))
    vwp = jnp.pad(v_w, ((0, 0), (WINDOW_2, 0), (0, 0), (0, 0)))

    slopes = alibi_slopes_2(NSA_HEADS).reshape(G, R)
    scale = Dh ** -0.5
    nb = s // QB
    qb = q.reshape(b, nb, QB, G, R, Dh).transpose(1, 0, 2, 3, 4, 5)
    gb = gates.reshape(b, nb, QB, 3, G, R).transpose(1, 0, 2, 3, 4, 5)
    bi = jnp.arange(b)[:, None, None, None]
    gi = jnp.arange(G)[None, :, None, None]
    jblk = jnp.arange(n_slc)

    def one(args):
        q_blk, g_blk, i = args
        q0 = i * QB
        t = q0 + jnp.arange(QB)
        tf = t.astype(jnp.float32)
        sc = jnp.einsum('bqgrd,bngd->bgrqn', q_blk, kc).astype(jnp.float32) * scale
        sc = sc - slopes[:, :, None, None] * (tf[:, None] - cmp_centre[None, :])
        valid = cmp_end[None, :] <= t[:, None]
        sc = jnp.where(valid, sc, NEG)
        has = jnp.any(valid, axis=-1).astype(jnp.float32)
        p_cmp = jax.nn.softmax(sc, axis=-1) * has[:, None]
        o_cmp = jnp.einsum('bgrqn,bngd->bqgrd', p_cmp.astype(vc.dtype), vc)
        imp = jnp.einsum('bgrqn,nj->bgqj', p_cmp, ov)
        cur = t // SLC_LEN
        forced = ((jblk[None, :] == 0) | (jblk[None, :] == cur[:, None])
                  | (jblk[None, :] == cur[:, None] - 1)).astype(jnp.float32)
        imp = jnp.where(jblk[None, :] > cur[:, None], NEG, imp + FORCE_BONUS * forced)
        _, sel = lax.top_k(imp, n_sel)
        ks = kb[bi, gi, sel]
        vs = vb[bi, gi, sel]
        kpos = sel[..., None] * SLC_LEN + jnp.arange(SLC_LEN)
        dist = (t[None, None, :, None, None] - kpos).astype(jnp.float32)
        sc = jnp.einsum('bqgrd,bgqnld->bgrqnl', q_blk, ks).astype(jnp.float32) * scale
        sc = sc - slopes[None, :, :, None, None, None] * dist[:, :, None]
        sc = jnp.where((dist >= 0)[:, :, None], sc, NEG)
        p = jax.nn.softmax(sc.reshape(b, G, R, QB, -1), axis=-1).reshape(sc.shape)
        o_slc = jnp.einsum('bgrqnl,bgqnld->bqgrd', p.astype(vs.dtype), vs)
        kw = lax.dynamic_slice_in_dim(kwp, q0, WINDOW_2 + QB, axis=1)
        vw = lax.dynamic_slice_in_dim(vwp, q0, WINDOW_2 + QB, axis=1)
        wpos = q0 - WINDOW_2 + jnp.arange(WINDOW_2 + QB)
        d = t[:, None] - wpos[None, :]
        sc = jnp.einsum('bqgrd,bsgd->bgrqs', q_blk, kw).astype(jnp.float32) * scale
        sc = sc - slopes[:, :, None, None] * d.astype(jnp.float32)
        sc = jnp.where((d >= 0) & (d < WINDOW_2) & (wpos[None, :] >= 0), sc, NEG)
        p = jax.nn.softmax(sc, axis=-1)
        o_win = jnp.einsum('bgrqs,bsgd->bqgrd', p.astype(vw.dtype), vw)
        return (g_blk[:, :, 0, :, :, None] * o_cmp + g_blk[:, :, 1, :, :, None] * o_slc
                + g_blk[:, :, 2, :, :, None] * o_win)

    out = lax.map(one, (qb, gb, jnp.arange(nb)))
    out = out.transpose(1, 0, 2, 3, 4, 5).reshape(b, s, C_MIX)
    return out @ w_out

def sq_relu_mlp(x, w1, w2):
    h = jax.nn.relu(x @ w1)
    return (h * h) @ w2

def _normal(k, shape, scale):
    return scale * jax.random.normal(k, shape, jnp.float32)

def second_inputs(seed: int = 0) -> dict:
    key = jax.random.key(seed)
    ks = jax.random.split(key, 24)
    nA, nC, D = N_A_LAYERS, N_C_LAYERS, D_MODEL
    gain = lambda k, shape: 1.0 + _normal(k, shape, 0.05)
    return {
        "x": _normal(ks[0], (BATCH, SEQ, D), 1.0),
        "norm_mix_pre": gain(ks[1], (DEPTH_2, D)),
        "norm_mix_post": gain(ks[2], (DEPTH_2, D)),
        "norm_mlp_pre": gain(ks[3], (DEPTH_2, D)),
        "norm_mlp_post": gain(ks[4], (DEPTH_2, D)),
        "mlp_w1": _normal(ks[5], (DEPTH_2, D, D_FF_2), D ** -0.5),
        "mlp_w2": _normal(ks[6], (DEPTH_2, D_FF_2, D), D_FF_2 ** -0.5),
        "a_w_in": _normal(ks[7], (nA, D, A_IN), D ** -0.5),
        "a_conv_w": _normal(ks[8], (nA, CONV_K, CONV_WIDTH), CONV_K ** -0.5),
        "a_q_norm": gain(ks[9], (nA, MLA_Q_RANK)),
        "a_w_q_up": _normal(ks[10], (nA, MLA_Q_RANK, MLA_HEADS * (MLA_NOPE + MLA_ROPE)), MLA_Q_RANK ** -0.5),
        "a_kv_norm": gain(ks[11], (nA, MLA_KV_RANK)),
        "a_w_kv_up": _normal(ks[12], (nA, MLA_KV_RANK, MLA_HEADS * (MLA_NOPE + MLA_V)), MLA_KV_RANK ** -0.5),
        "a_w_out": _normal(ks[13], (nA, A_MIX, D), A_MIX ** -0.5),
        "c_w_in": _normal(ks[14], (nC, D, C_IN), D ** -0.5),
        "c_cmp_pe_k": _normal(ks[15], (nC, CMP_LEN, NSA_DH), 0.1),
        "c_cmp_w1_k": _normal(ks[16], (nC, CMP_LEN, NSA_DH, NSA_DH), (CMP_LEN * NSA_DH) ** -0.5),
        "c_cmp_w2_k": _normal(ks[17], (nC, NSA_DH, NSA_DH), NSA_DH ** -0.5),
        "c_cmp_pe_v": _normal(ks[18], (nC, CMP_LEN, NSA_DH), 0.1),
        "c_cmp_w1_v": _normal(ks[19], (nC, CMP_LEN, NSA_DH, NSA_DH), (CMP_LEN * NSA_DH) ** -0.5),
        "c_cmp_w2_v": _normal(ks[20], (nC, NSA_DH, NSA_DH), NSA_DH ** -0.5),
        "c_w_out": _normal(ks[21], (nC, C_MIX, D), C_MIX ** -0.5),
    }

def second_block(x, norm_mix_pre, norm_mix_post, norm_mlp_pre, norm_mlp_post, mlp_w1, mlp_w2,
              a_w_in, a_conv_w, a_q_norm, a_w_q_up, a_kv_norm, a_w_kv_up, a_w_out,
              c_w_in, c_cmp_pe_k, c_cmp_w1_k, c_cmp_w2_k, c_cmp_pe_v, c_cmp_w1_v, c_cmp_w2_v,
              c_w_out):
    for layer in range(DEPTH_2):
        i = layer // 2
        h = rms_norm_2(x, norm_mix_pre[layer])
        if layer % 2 == 0:
            m = mixer_a(h, a_w_in[i], a_conv_w[i], a_q_norm[i], a_w_q_up[i],
                        a_kv_norm[i], a_w_kv_up[i], a_w_out[i])
        else:
            m = mixer_c(h, c_w_in[i], c_cmp_pe_k[i], c_cmp_w1_k[i], c_cmp_w2_k[i],
                        c_cmp_pe_v[i], c_cmp_w1_v[i], c_cmp_w2_v[i], c_w_out[i])
        x = x + rms_norm_2(m, norm_mix_post[layer])
        h = rms_norm_2(x, norm_mlp_pre[layer])
        x = x + rms_norm_2(sq_relu_mlp(h, mlp_w1[layer], mlp_w2[layer]), norm_mlp_post[layer])
    return x


def setup_inputs(seed=0):
    out = dict(first_inputs(seed))
    for name, value in second_inputs(seed + 1).items():
        if name != "x":
            out[name + "_2"] = value
    return out


def reference(
    x, meta_tokens, norm_mix, w_in, lambda_q1, lambda_k1, lambda_q2, lambda_k2, subln_gain,
    sink_logits, w_branch_a, w_branch_b, w_out, norm_ffn, w_ff_gate, w_ff_up, w_ff_down,
    norm_final, norm_mix_pre_2, norm_mix_post_2, norm_mlp_pre_2, norm_mlp_post_2, mlp_w1_2,
    mlp_w2_2, a_w_in_2, a_conv_w_2, a_q_norm_2, a_w_q_up_2, a_kv_norm_2, a_w_kv_up_2, a_w_out_2,
    c_w_in_2, c_cmp_pe_k_2, c_cmp_w1_k_2, c_cmp_w2_k_2, c_cmp_pe_v_2, c_cmp_w1_v_2,
    c_cmp_w2_v_2, c_w_out_2,
):
    x = first_block(
        x, meta_tokens, norm_mix, w_in, lambda_q1, lambda_k1, lambda_q2, lambda_k2, subln_gain,
        sink_logits, w_branch_a, w_branch_b, w_out, norm_ffn, w_ff_gate, w_ff_up, w_ff_down,
        norm_final,
    )
    return second_block(
        x, norm_mix_pre_2, norm_mix_post_2, norm_mlp_pre_2, norm_mlp_post_2, mlp_w1_2, mlp_w2_2,
        a_w_in_2, a_conv_w_2, a_q_norm_2, a_w_q_up_2, a_kv_norm_2, a_w_kv_up_2, a_w_out_2,
        c_w_in_2, c_cmp_pe_k_2, c_cmp_w1_k_2, c_cmp_w2_k_2, c_cmp_pe_v_2, c_cmp_w1_v_2,
        c_cmp_w2_v_2, c_w_out_2,
    )


_drawn_inputs = setup_inputs


def setup_inputs(seed=0):
    import zlib

    import numpy as np

    out = dict(_drawn_inputs(seed))
    spreads = {}
    factors = {'subln_gain': 3.862,
     'sink_logits': 8.0,
     'a_q_norm_2': 8.0,
     'a_kv_norm_2': 4.289,
     'c_cmp_pe_k_2': 8.0}
    for name, (base, spread) in spreads.items():
        noise = np.random.default_rng([zlib.crc32(name.encode()), seed]).standard_normal(out[name].shape)
        drawn = base * np.exp(spread * noise) if base else spread * noise
        out[name] = __import__('jax').numpy.asarray(drawn.astype(out[name].dtype))
    for name, factor in factors.items():
        out[name] = (out[name] * factor).astype(out[name].dtype)
    return out
```

```python
from contextlib import ExitStack

import numpy as np

import concourse.bass as bass
from concourse import mybir
from concourse.alu_op_type import AluOpType as ALU

ACT = mybir.ActivationFunctionType
AX = mybir.AxisListType
F32 = mybir.dt.float32
F16 = mybir.dt.float16
BF16 = mybir.dt.bfloat16

P = 128
T = 512
NQ = T // P
M = 16
TM = T + M
D = 1024
KD = D // P
HD = 64
FF1 = 2816
KFF1 = FF1 // P
FF2 = 4096
KFF2 = FF2 // P
EPS = 1e-6
WS = 64.0
NEG = -1e30
NCMP = 31
NCP = 32
CL = 32
LINIT = 0.2
MLA_SCALE = 96.0 ** -0.5

TPU = 16
UW = TPU * P
RAW = 3
WR = 4
LOOK = 2


class Stage:

    def __init__(self, name, kind, n, k, width, o0, tau0):
        self.name, self.kind, self.n, self.k, self.width, self.o0, self.tau0 = name, kind, n, k, width, o0, tau0

    def tile(self, j, k):
        return self.tau0 + (j * self.k + k if self.kind == "T" else k * self.width)


class Plan:

    def __init__(self):
        self.st, self.order = {}, []
        self.o = self.tau = self.ms = 0
        self.out_ms, self.unit_ms, self.out_tau, self.marks = [], {}, [], set()
        for name, kind, n, k, width in STAGES:
            if kind == "N":
                self.tau += (-self.tau) % width
            s = Stage(name, kind, n, k, width, self.o, self.tau)
            self.st[name] = s
            self.order.append(s)
            if kind == "T":
                for j in range(n):
                    for kk in range(k):
                        self.step(self.tau, 1, kk == k - 1)
            else:
                for kk in range(k):
                    for t in range(n):
                        last = kk == k - 1
                        ends = t == n - 1 and (self.tau + width) % TPU == 0
                        if last or ends:
                            self.ms += 1
                            self.marks.add((self.tau, t))
                        if last:
                            self.out_ms.append(self.ms)
                            self.out_tau.append(self.tau + width - 1)
                        if ends:
                            self.unit_ms[self.tau // TPU] = self.ms
                    self.tau += width
                self.o += n
        self.n_units = -(-self.tau // TPU)
        self.r = {}
        at = 0
        for name, n in RHS:
            self.r[name] = at
            at += n
        self.s = {}
        at = 0
        for name, n in SRC:
            self.s[name] = at
            at += n
        self.q = {}
        at = 0
        for name, n in SQUARES:
            self.q[name] = at
            at += n

    def step(self, tau, width, last):
        ends = (tau + width) % TPU == 0
        if last or ends:
            self.ms += 1
            self.marks.add((tau, 0))
        if last:
            self.out_ms.append(self.ms)
            self.out_tau.append(tau)
            self.o += 1
        if ends:
            self.unit_ms[tau // TPU] = self.ms
        self.tau += width


STAGES = (
    [("qa", "T", 4, KD, 1), ("ka", "T", 4, KD, 1), ("va", "N", NQ, KD, 4), ("qb", "T", 4, KD, 1),
     ("kb", "T", 1, KD, 1), ("vb", "N", NQ, KD, 1)]
    + [x for n in range(KD) for x in ((f"mrg_ga{n}", "T", 1, KD, 1), (f"mrg_gb{n}", "T", 1, KD, 1),
                                      (f"mrg_a{n}", "T", 1, 4, 1), (f"mrg_b{n}", "T", 1, 4, 1))]
    + [("wo", "T", KD, KD, 1), ("ffgu", "T", 2 * KFF1, KD, 1), ("ffd", "T", KD, KFF1, 1),
       ("cv", "T", 12, KD, 1), ("cq", "T", 6, KD, 1), ("ckv", "T", 2, KD, 1), ("kr", "T", 1, KD, 1),
       ("qn", "T", 4, 6, 1), ("qr", "T", 2, 6, 1), ("kn", "T", 4, 2, 1), ("vm", "N", NQ, 2, 4),
       ("awo", "T", KD, KD, 1), ("up0", "T", KFF2, KD, 1), ("dn0", "T", KD, KFF2, 1),
       ("kc", "T", 2, KD, 1), ("vc", "T", 2, KD, 1), ("q2", "T", 8, KD, 1), ("ks", "T", 2, KD, 1),
       ("kw", "T", 2, KD, 1), ("vv", "N", NQ, KD, 4), ("gt", "N", NQ, KD, 1),
       ("ck1", "T", 1, CL, 1), ("cv1", "T", 1, CL, 1), ("ck2", "T", 1, 1, 1), ("cv2", "T", 1, 1, 1),
       ("cwo", "T", KD, KD, 1), ("up1", "T", KFF2, KD, 1), ("dn1", "T", KD, KFF2, 1)]
)
RHS = [("x0", 8), ("ya", 8), ("yb", 4), ("mrg", 8), ("x1", 8), ("ff", KFF1), ("xb", 8), ("conv", 4),
       ("cq", 6), ("ckv", 2), ("ymla", 4), ("p1", 8), ("h0", KFF2), ("p2", 8), ("z", 4), ("pe", 1),
       ("hid", 2), ("ynsa", 8), ("p3", 8), ("h1", KFF2)]
SRC = [("mrg", 8), ("ff", KFF1), ("xb", 8), ("conv", 4), ("p1", 8), ("h0", KFF2), ("p2", 8), ("hid", 2),
       ("p3", 8), ("h1", KFF2), ("out", 8)]
SQUARES = [("x0", 8), ("x1", 8), ("x2", 8), ("xb", 8), ("cq", 6), ("ckv", 2), ("ma", 8), ("p1", 8),
           ("mb", 8), ("p2", 8), ("mc", 8), ("p3", 8), ("md", 8)]
NORM = {n: i for i, (n, _) in enumerate(SQUARES)}
PL = Plan()


class Task:

    def __init__(self, kind, qi, h, kb, group, col, dv, j, last, s=0, b=0):
        self.kind, self.qi, self.h = kind, qi, h
        self.s, self.b = s, b
        self.kb = kb
        self.group, self.j, self.last = group, j, last
        self.col, self.dv = col, dv


class Phase:

    def __init__(self, name, tasks, t0, g0, i0, r0, y_after, slots):
        self.name, self.tasks, self.t0, self.g0, self.slots = name, tasks, t0, g0, slots
        self.items = []
        ny = 0
        self.y_at = {}
        for n, t in enumerate(tasks):
            t.n, t.t = n, t0 + n
            t.item = i0 + len(self.items)
            self.items.append(("P", t.t))
            for y, after in y_after:
                if n == min(after + 4, len(tasks) - 1):
                    self.y_at.setdefault(n, []).append((i0 + len(self.items), y))
                    self.items.append(("Y", r0 + y))
        self.n_groups = tasks[-1].group + 1
        self.t1, self.g1, self.i1 = t0 + len(tasks), g0 + self.n_groups, i0 + len(self.items)


def key_blocks(i):
    return list(range(max(0, i - 1), min(NQ, i + 2)))


def make_phases():
    out, t, g, i = {}, 0, 0, 0
    diff = []
    for qi in range(NQ):
        for h in range(4):
            for s in range(2):
                diff.append(Task(kind="diff", qi=qi, h=h, s=s, kb=list(range(NQ)), group=qi * 2 + h // 2,
                                 col=((h % 2) * 2 + s) * P, dv=P, j=(h % 2) * 2 + s, last=(h % 2 == 1 and s == 1)))
    y = [(k, 4 * k + 3) for k in range(8)]
    out["diff"] = p = Phase("diff", diff, t, g, i, PL.r["ya"], y, 2)
    t, g, i = p.t1, p.g1, p.i1
    for name, r in (("win", "yb"), ("mla", "ymla")):
        tasks = []
        for qi in range(NQ):
            for h in range(8):
                kb = key_blocks(qi) if name == "win" else list(range(qi + 1))
                tasks.append(Task(kind=name, qi=qi, h=h, kb=kb, group=qi, col=h * HD, dv=HD, j=h, last=h == 7))
        y = [(k, 8 * k + 7) for k in range(4)]
        out[name] = p = Phase(name, tasks, t, g, i, PL.r[r], y, 4)
        t, g, i = p.t1, p.g1, p.i1
    tasks, y = [], []
    for qi in range(NQ):
        tasks.append(Task(kind="cmp", qi=qi, h=0, kb=[0, 1, 2, 3], group=qi * 6 + 1, col=0, dv=HD, j=0, last=True))
        for b in range(2):
            for h in range(16):
                tasks.append(Task(kind="nsa", b=b, qi=qi, h=h, kb=list(range(qi + 1)), group=qi * 6 + 2 + b * 2 + h // 8,
                                  col=(h % 8) * HD, dv=HD, j=h % 8, last=h % 8 == 7))
                if b and h % 8 == 7:
                    y.append((qi * 2 + h // 8, len(tasks) - 1))
    out["nsa"] = Phase("nsa", tasks, t, g, i, PL.r["ynsa"], y, 4)
    return out


PH = make_phases()
ITEMS = [x for p in PH.values() for x in p.items]


def pt_on_dve(t):
    return t % 2 == 0


def slopes(n):
    return (2.0 ** (-8.0 * np.arange(1, n + 1) / n)).astype(np.float32)


CONST = {}


def const_columns():
    p = np.arange(P)
    c = np.arange(896)
    parts = []

    def put(name, a):
        a = np.asarray(a, np.float32).reshape(P, -1)
        at = sum(x.shape[1] for x in parts)
        CONST[name] = (at, at + a.shape[1])
        parts.append(a)

    put("ident", np.eye(P))
    swap = np.zeros((P, P))
    for m in range(P):
        if m % 32 < 16:
            swap[m + 16, m] = -1
        else:
            swap[m - 16, m] = 1
    put("swap", swap)
    dist = p[:, None] + 384 - c[None, :]
    put("dist", -np.abs(dist))
    put("band", np.where(np.abs(dist) > 128, NEG, 0.0))
    put("causal", np.where(p[None, :] > p[:, None], NEG, 0.0))
    sl = slopes(16).astype(np.float64) * 64
    pieces = []
    for _ in range(3):
        h = sl.astype(np.float16).astype(np.float64)
        pieces.append(h)
        sl = sl - h
    aug = np.zeros((P, 16, P))
    for k in range(3):
        aug[k] = pieces[k][:, None]
    put("aug", aug)
    rel = np.zeros((P, 896))
    rel[:3] = (c - 384) / 64.0
    put("rel", rel)
    put("has", (p[:, None] + P * np.arange(NQ)[None, :] >= CL - 1).astype(np.float32))
    half = 16
    inv = (np.float32(10000.0) ** (-np.arange(half, dtype=np.float32) / np.float32(half))).astype(np.float32)
    ang = np.arange(T, dtype=np.float32)[None, :] * inv[p % 16][:, None]
    put("cos", np.cos(ang))
    put("sin", np.sin(ang))
    starts = np.arange(NCMP) * 16
    centre = starts + (CL - 1) / 2.0
    bias = np.full((P, NQ, 16, NCP), NEG, np.float32)
    for i in range(NQ):
        t = p + P * i
        for h in range(16):
            v = -slopes(16)[h] * (t[:, None] - centre[None, :]).astype(np.float32)
            ok = (starts + CL - 1)[None, :] <= t[:, None]
            bias[:, i, h, :NCMP] = np.where(ok, v, NEG)
    put("cmpbias", bias)
    return np.ascontiguousarray(np.concatenate(parts, axis=1))


CONSTANTS = const_columns()
KEEP_TO = CONST["has"][1]

PARAM, _at = {}, 0
for _name, _n in (("g_mix", 8), ("g_ffn", 8), ("g_fin", 8), ("g_pre0", 8), ("g_post0", 8), ("g_mpre0", 8),
                  ("g_mpost0", 8), ("g_pre1", 8), ("g_post1", 8), ("g_mpre1", 8), ("g_mpost1", 8),
                  ("g_sub", 1), ("g_cq", 6), ("g_ckv", 2), ("conv", 12), ("sink", 8), ("lam", 256),
                  ("pe", 64)):
    PARAM[_name] = (_at, _at + _n)
    _at += _n
N_PARAM = _at


def y_parts(ph, y, dst, ps):
    if ph.name in ("diff", "nsa"):
        qi, half = y // 2, y % 2
        n = 2 if ph.name == "diff" else 4
        k = half * n
    else:
        qi, k, n = y, 0, 4
    return (dst[:, k:k + n, qi * P:(qi + 1) * P], ps[:, 0:n * P].rearrange("p (a b) -> p a b", a=n))


def group_ends(ph, n):
    if n < 0 or not ph.tasks[n].last:
        return []
    g = ph.tasks[n].group
    return [g - 1, g] if ph.tasks[n].kind == "cmp" else [g]


def items_done(t):
    for ph in PH.values():
        if ph.t0 <= t < ph.t1:
            return ph.tasks[t - ph.t0].item + 1
    raise ValueError(t)


def y_item(ph, y):
    return [i for n in sorted(ph.y_at) for i, yy in ph.y_at[n] if yy == y][0]


def build_program(nc, x_in, stream, consts, params, out):
    ctx = ExitStack()
    with ctx:
        def sb(name, shape, dt=F32):
            return ctx.enter_context(nc.sbuf_tensor(name, shape, dt))

        def sem(name):
            return ctx.enter_context(nc.semaphore(name))

        w_raw = sb("w_raw", [P, RAW, UW])
        w_hi = sb("w_hi", [P, WR, UW], F16)
        w_lo = sb("w_lo", [P, WR, UW], F16)
        X = sb("X", [P, KD, TM])
        xx = sb("xx", [P, KD, 2, TM], F16)
        xx32 = xx[:, :, :, :].rearrange("p a b c -> p (a b c)").bitcast(F32).rearrange("p (a b) -> p a b", a=KD)
        xa = [xx[:, :, 0, :], xx[:, :, 1, :]]
        sq = sb("sq", [P, 2, TM])
        acc = sb("acc", [P, TM])
        rs = sb("rs", [P, TM])
        rn = sb("rn", [P, NQ + 1])
        rsq = sb("rsq", [P, T])
        rnk = sb("rnk", [P, NQ])
        tmp = sb("tmp", [P, 4, T])
        src = sb("src", [P, 2, T])
        ident = sb("ident", [P, P])
        swap = sb("swap", [P, P])
        identb = sb("identb", [P, P], BF16)
        sident = sb("sident", [P, 8, P], F16)
        dist = sb("dist", [P, 896], F16)
        band = sb("band", [P, 896], BF16)
        causal = sb("causal", [P, P], BF16)
        aug = sb("aug", [4, 16, P], F16)
        rel = sb("rel", [4, 896], F16)
        has = sb("has", [P, NQ])
        ones = sb("ones", [P, P])
        epsb = sb("epsb", [P, 2])
        half_neg = sb("half_neg", [P, 2])
        par = sb("par", [P, N_PARAM])
        lam = sb("lam", [P, 4])
        nsink = sb("nsink", [P, 8])
        nmax = sb("nmax", [P, 4, 8])
        sums = sb("sums", [P, 4, 8])
        scale8 = sb("scale8", [P, 2, 8])
        sgn = sb("sgn", [P, 4])
        ssq = sb("ssq", [P, 2, 6])
        sink_e = sb("sink_e", [P, 8])
        cst = sb("cst", [P, 3, 16])
        ARENA = 19800
        arena = sb("arena", [P, ARENA])
        ar16 = arena[:, :].bitcast(F16)

        def view(at, shape, dt=F32):
            n = int(np.prod(shape))
            cols = n if dt == F32 else (n + 1) // 2
            assert at + cols <= ARENA, (at, shape)
            v = arena[:, at:at + n] if dt == F32 else ar16[:, 2 * at:2 * at + n]
            if len(shape) == 2:
                v = v.rearrange("p (a b) -> p a b", a=shape[0])
            if len(shape) == 3:
                v = v.rearrange("p (a b c) -> p a b c", a=shape[0], b=shape[1])
            return v, at + cols

        p_sb, at = view(0, [3, TM])
        pt_sb, at = view(at, [2, 5, P])
        o_nat, att0 = view(at, [4, T])
        qa, at = view(att0, [4, T])
        ka, at = view(at, [4, TM])
        va, at = view(at, [NQ + 1, T])
        qb, at = view(at, [4, T])
        kb_, at = view(at, [TM])
        vb, at = view(at, [NQ + 1, P])
        ya_, yb_ = [None, None], [None, None]
        ya_[0], at = view(at, [4, T], F16)
        ya_[1], at = view(at, [4, T], F16)
        yb_[0], at = view(at, [4, T], F16)
        yb_[1], at = view(at, [4, T], F16)
        mg, ffh = [None, None], [None, None]
        mg[0], at = view(0, [KD, T], F16)
        mg[1], at = view(at, [KD, T], F16)
        ffh[0], at = view(0, [KFF2, T], F16)
        ffh[1], at = view(at, [KFF2, T], F16)
        stage_c, _ = view(ARENA - KEEP_TO, [KEEP_TO])
        mx, cqs, cks = [None, None], [None, None], [None, None]
        cos, at = view(att0, [T])
        sin, at = view(at, [T])
        mx[0], at = view(at, [KD, T], F16)
        mx[1], at = view(at, [KD, T], F16)
        cq0 = at
        cqs[0], at = view(at, [6, T], F16)
        cqs[1], at = view(at, [6, T], F16)
        vm, _ = view(cq0, [NQ, T])
        cks[0], at = view(at, [2, T], F16)
        cks[1], at = view(at, [2, T], F16)
        vpad, _ = view(at, [2 + T])
        qn, at = view(at, [4, T])
        qr, at = view(at, [3, T])
        kn, at = view(at, [4, T])
        z, pe_s, hid = [None, None], [None, None], [None, None]
        q2, at = view(att0, [8, T])
        m_att = q2
        ks, at = view(at, [2, T])
        kw, at = view(at, [2, T])
        vv, at = view(at, [NQ, T])
        gates, at = view(at, [NQ, 48])
        kct, at = view(at, [4, NCP])
        vcbd, at = view(at, [4, 4 * HD])
        cbias, at = view(at, [NQ, T])
        for i in range(2):
            z[i], at = view(at, [4, T], F16)
            pe_s[i], at = view(at, [64], F16)
            hid[i], at = view(at, [2, 64], F16)

        pS = ctx.enter_context(nc.psum_tensor("pS", [P, 4, 512], F32))
        pT = ctx.enter_context(nc.psum_tensor("pT", [P, 2, 512], F32))
        pO = ctx.enter_context(nc.psum_tensor("pO", [P, 2, 512], F32))

        x_loaded = sem("x_loaded")
        par_loaded = sem("par_loaded")
        const_loaded = sem("const_loaded")
        table_loaded = sem("table_loaded")
        raw_loaded = [sem(f"raw_loaded{i}") for i in range(RAW)]
        basics_ready = sem("basics_ready")
        tables_ready = sem("tables_ready")
        hi_split = sem("hi_split")
        lo_split = sem("lo_split")
        mm_done = sem("mm_done")
        evicted = sem("evicted")
        computed = sem("computed")
        rhs_hi = sem("rhs_hi")
        rhs_ready = sem("rhs_ready")
        squared = sem("squared")
        sq_summed = sem("sq_summed")
        norm_mm = sem("norm_mm")
        norm_root_ = sem("norm_root")
        dve_chain = sem("dve_chain")
        tanh_in = sem("tanh_in")
        act_out = sem("act_out")
        scores = sem("scores")
        maxed = sem("maxed")
        probs = sem("probs")
        transposed = sem("transposed")
        pt_dve = sem("pt_dve")
        pt_act = sem("pt_act")
        av_done = sem("av_done")
        grp_out = sem("grp_out")
        y_done = sem("y_done")
        sink_exp = sem("sink_exp")
        pow_in = sem("pow_in")
        pow_out = sem("pow_out")
        rope_mm = sem("rope_mm")
        rope_done = sem("rope_done")
        out_stored = sem("out_stored")

        n_dve = [sum(pt_on_dve(t) for t in range(n)) for n in range(PH["nsa"].t1 + 1)]
        n_act = [n - n_dve[n] for n in range(PH["nsa"].t1 + 1)]
        S = PL.st

        def pcol(name, k=0, n=1):
            a = PARAM[name][0]
            return par[:, a + k:a + k + n]

        def p_parts(ph, t):
            pt, pb, n = pt_sb[:, t.t % 2], t.item % 2, len(t.kb)
            parts = [(pt[:, 0:n, :], pT[:, pb, 0:n * P].rearrange("p (a b) -> p a b", a=n))]
            if t.kind == "diff":
                parts.append((pt[0:M, 4, :], pS[0:M, (t.t % 2) * 2 + 1, P:2 * P]))
            elif t.kind == "win":
                parts.append((pt[0:M, n, :], pT[0:M, pb, n * P:(n + 1) * P]))
            return parts

        def m_view(m, n):
            return m_att[:, n, :] if m == "mc" else xx32[:, n, 0:T]

        def score_view(ph, t):
            w = 4 // ph.slots
            sl = (t.t % ph.slots) * w
            if t.kind == "diff":
                return pS[:, sl:sl + 2, :].rearrange("p a b -> p (a b)")[:, 0:TM]
            if t.kind == "cmp":
                return pS[:, sl, :]
            return pS[:, sl, 0:len(t.kb) * P + (M if t.kind == "win" else 0)]

        block = ctx.enter_context(nc.Block())

        @block.gpsimd
        def _(pool):
            pool.wait_ge(basics_ready, 1)
            for g in range(PH["diff"].n_groups):
                pool.wait_ge(pow_in, g + 1)
                pool.tensor_tensor(ssq[:, g % 2, 2:4], ssq[:, g % 2, 0:2], half_neg[:, :], ALU.pow).then_inc(pow_out, 1)

        @block.tensor
        def _(pe):
            unit = [-1]

            def weights(tau, n=1):
                u = tau // TPU
                if u != unit[0]:
                    pe.wait_ge(lo_split, u + 1)
                    unit[0] = u
                a = (tau % TPU) * P
                return w_hi[:, u % WR, a:a + n * P], w_lo[:, u % WR, a:a + n * P]

            def bank_free(o):
                if o >= 4:
                    pe.wait_ge(evicted, o - 3)

            def out_T(s, j, rhs, n_cols=T, meta=None, rhs_wait=None):
                o = s.o0 + j
                bank_free(o)
                ps = pS[:, o % 4, 0:n_cols]
                for k in range(s.k):
                    if rhs_wait is not None:
                        pe.wait_ge(rhs_ready, rhs_wait + k + 1)
                    tau = s.tile(j, k)
                    wh, wl = weights(tau)
                    ah, al = rhs(0, k), rhs(1, k)
                    f, l = k == 0, k == s.k - 1
                    if meta is not None:
                        mps, mr = meta
                        pe.matmul(mps, wh, mr(0, k), start=f, stop=False)
                        pe.matmul(mps, wh, mr(1, k), start=False, stop=False)
                        pe.matmul(mps, wl, mr(0, k), start=False, stop=l)
                    pe.matmul(ps, wh, ah, start=f, stop=False)
                    pe.matmul(ps, wh, al, start=False, stop=False)
                    mm = pe.matmul(ps, wl, ah, start=False, stop=l)
                    if (tau, 0) in PL.marks:
                        mm.then_inc(mm_done, 1)

            def out_N(s, lhs, meta=None):
                pe.wait_ge(evicted, s.o0)
                w = s.width * P
                for k in range(s.k):
                    tau = s.tile(0, k)
                    wh, wl = weights(tau, s.width)
                    f, l = k == 0, k == s.k - 1
                    if meta is not None:
                        pe.matmul(meta, lhs(0, k)[:, T:TM], wh, start=f, stop=False)
                        pe.matmul(meta, lhs(0, k)[:, T:TM], wl, start=False, stop=False)
                        pe.matmul(meta, lhs(1, k)[:, T:TM], wh, start=False, stop=l)
                    for t in range(NQ):
                        ps = pS[:, (s.o0 + t) % 4, 0:w]
                        a = slice(t * P, (t + 1) * P)
                        pe.matmul(ps, lhs(0, k)[:, a], wh, start=f, stop=False)
                        pe.matmul(ps, lhs(0, k)[:, a], wl, start=False, stop=False)
                        mm = pe.matmul(ps, lhs(1, k)[:, a], wh, start=False, stop=l)
                        if (tau, t) in PL.marks:
                            mm.then_inc(mm_done, 1)

            def norm_sum(name, meta=False, natural=False):
                pe.wait_ge(sq_summed, PL.q[name] + dict(SQUARES)[name])
                if meta:
                    pe.matmul(pO[:, 1, 8:8 + M], ones[:, :], acc[:, T:TM], start=True, stop=True)
                    pe.matmul(pO[0:M, 1, 4:5], acc[:, T:TM], ones[:, 0:1], start=True, stop=True)
                if natural:
                    for t in range(NQ):
                        pe.matmul(pO[:, 1, t:t + 1], acc[:, t * P:(t + 1) * P], ones[:, 0:1], start=True, stop=True)
                pe.matmul(pT[:, 1, :], ones[:, :], acc[:, 0:T], start=True, stop=True).then_inc(norm_mm, 1)

            def moved_pt(t):
                if pt_on_dve(t):
                    pe.wait_ge(pt_dve, n_dve[t + 1])
                else:
                    pe.wait_ge(pt_act, n_act[t + 1])

            def item_free(i):
                if i < 2:
                    return
                kind, v = ITEMS[i - 2]
                if kind == "Y":
                    pe.wait_ge(rhs_ready, v + 1)
                else:
                    moved_pt(v)

            def score(ph, t):
                if t.t - ph.slots >= ph.t0:
                    pe.wait_ge(probs, t.t - ph.slots + 1)
                sl = (t.t % ph.slots) * (4 // ph.slots)
                qs = slice(t.qi * P, (t.qi + 1) * P)
                n = len(t.kb) * P
                k0 = t.kb[0] * P
                c0 = 384 - P * t.qi + k0
                if t.kind == "diff":
                    d = slice(t.s * HD, (t.s + 1) * HD)
                    pe.matmul(pS[:, sl, :], qa[d, t.h, qs], ka[d, t.h, 0:T], start=True, stop=False)
                    pe.matmul(pS[:, sl, :], sident[:, 2 * t.h + 1, :], dist[:, c0:c0 + n], start=False, stop=True)
                    if t.t - ph.slots >= ph.t0:
                        moved_pt(t.t - ph.slots)
                    mm = pe.matmul(pS[:, sl + 1, 0:M], qa[d, t.h, qs], ka[d, t.h, T:TM], start=True, stop=True)
                elif t.kind == "win":
                    g = t.h // 4
                    d = slice(g * HD, (g + 1) * HD)
                    q = qb[d, t.h % 4, qs]
                    pe.matmul(pS[:, sl, n:n + M], q, kb_[d, T:TM], start=True, stop=True)
                    pe.matmul(pS[:, sl, 0:n], q, kb_[d, k0:k0 + n], start=True, stop=False)
                    pe.matmul(pS[:, sl, 0:n], sident[:, t.h, :], dist[:, c0:c0 + n], start=False, stop=False)
                    mm = pe.matmul(pS[:, sl, 0:n], identb[:, :], band[:, c0:c0 + n], start=False, stop=True)
                elif t.kind == "mla":
                    d = slice((t.h % 2) * HD, (t.h % 2 + 1) * HD)
                    r = slice((t.h % 4) * 32, (t.h % 4 + 1) * 32)
                    pe.matmul(pS[:, sl, 0:n], qn[d, t.h // 2, qs], kn[d, t.h // 2, 0:n], start=True, stop=False)
                    pe.matmul(pS[:, sl, 0:n], qr[r, t.h // 4, qs], qr[r, 2, 0:n], start=False, stop=False)
                    mm = pe.matmul(pS[:, sl, n - P:n], identb[:, :], causal[:, :], start=False, stop=True)
                elif t.kind == "cmp":
                    for h in range(16):
                        g, r = h // 4, h % 4
                        mm = pe.matmul(pS[:, sl, h * NCP:(h + 1) * NCP], q2[:, (g // 2) * 4 + r, qs], kct[:, g, :],
                                       start=True, stop=True)
                else:
                    g, r = t.h // 4, t.h % 4
                    d = slice((g % 2) * HD, (g % 2 + 1) * HD)
                    k = (ks, kw)[t.b]
                    pe.matmul(pS[:, sl, 0:n], q2[d, (g // 2) * 4 + r, qs], k[d, g // 2, 0:n], start=True, stop=False)
                    pe.matmul(pS[:, sl, 0:n], aug[0:3, t.h, :], rel[0:3, c0:c0 + n], start=False, stop=False)
                    mm = pe.matmul(pS[:, sl, n - P:n], identb[:, :], causal[:, :], start=False, stop=True)
                mm.then_inc(scores, 1)

            def transpose_p(ph, t):
                pe.wait_ge(probs, t.t + 1)
                item_free(t.item)
                pb = t.item % 2
                p = p_sb[:, t.t % 3, :]
                n = len(t.kb) * P
                if t.kind == "diff":
                    pe.transpose(pS[0:M, (t.t % 2) * 2 + 1, P:2 * P], p[:, n:n + M], ident[:, :])
                elif t.kind == "win":
                    pe.transpose(pT[0:M, pb, n:n + P], p[:, n:n + M], ident[:, :])
                for b in range(len(t.kb)):
                    mm = pe.transpose(pT[:, pb, b * P:(b + 1) * P], p[:, b * P:(b + 1) * P], ident[:, :])
                mm.then_inc(transposed, 1)

            def attend(ph, t):
                moved_pt(t.t)
                G = ph.g0 + t.group
                if t.j == 0 and G >= 2:
                    pe.wait_ge(grp_out, G - 1)
                pt = pt_sb[:, t.t % 2]
                if t.kind == "cmp":
                    for g in range(4):
                        mm = pe.matmul(pO[:, (G - 1 + g // 2) % 2, (g % 2) * 256:(g % 2 + 1) * 256], pt[:, g, :],
                                       vcbd[:, g, :], start=True, stop=True)
                    mm.then_inc(av_done, 2)
                    return
                o = pO[:, G % 2, t.col:t.col + t.dv]
                nb = len(t.kb)
                if t.kind == "diff":
                    c = slice(t.h * P, (t.h + 1) * P)
                    blocks = [(pt[:, b, :], va[:, k, c]) for b, k in enumerate(t.kb)] + [(pt[0:M, 4, :], va[0:M, NQ, c])]
                elif t.kind == "win":
                    c = slice((t.h // 4) * HD, (t.h // 4 + 1) * HD)
                    blocks = [(pt[:, b, :], vb[:, k, c]) for b, k in enumerate(t.kb)] + [(pt[0:M, nb, :], vb[0:M, NQ, c])]
                elif t.kind == "mla":
                    c = slice(t.h * HD, (t.h + 1) * HD)
                    blocks = [(pt[:, b, :], vm[:, k, c]) for b, k in enumerate(t.kb)]
                else:
                    c = t.b * 256 + (t.h // 4) * HD
                    blocks = [(pt[:, b, :], vv[:, k, c:c + HD]) for b, k in enumerate(t.kb)]
                for b, (l, r) in enumerate(blocks):
                    mm = pe.matmul(o, l, r, start=b == 0, stop=b == len(blocks) - 1)
                if t.last:
                    mm.then_inc(av_done, 1)

            def transpose_y(ph, item, y):
                item_free(item)
                if ph.name == "diff":
                    pe.wait_ge(y_done, y + 1)
                elif ph.name == "nsa":
                    pe.wait_ge(y_done, PH["diff"].n_groups + y + 1)
                else:
                    pe.wait_ge(grp_out, ph.g0 + y + 1)
                for b in range(2 if ph.name == "diff" else 4):
                    mm = pe.transpose(pT[:, item % 2, b * P:(b + 1) * P], o_nat[:, y % 4, b * P:(b + 1) * P], ident[:, :])
                mm.then_inc(transposed, 1)

            def attention(ph):
                ts = ph.tasks
                score(ph, ts[0])
                score(ph, ts[1])
                for n, t in enumerate(ts):
                    transpose_p(ph, t)
                    if n + 2 < len(ts):
                        score(ph, ts[n + 2])
                    if n:
                        attend(ph, ts[n - 1])
                    if n == len(ts) - 1:
                        attend(ph, t)
                    for item, y in ph.y_at.get(n, []):
                        transpose_y(ph, item, y)
                pe.wait_ge(probs, ph.t1)

            def of(a):
                return lambda q, k: a[q][:, k, 0:T]

            xr = of(xa)
            xm = lambda q, k: xa[q][:, k, T:TM]
            full = lambda q, k: xa[q][:, k, :]
            pe.wait_ge(basics_ready, 1)
            out_T(S["qa"], 0, xr, rhs_wait=PL.r["x0"])
            norm_sum("x0", meta=True, natural=True)
            for j in range(1, 4):
                out_T(S["qa"], j, xr)
            pe.wait_ge(norm_root_, 1)
            for j in range(4):
                out_T(S["ka"], j, xr, meta=(pT[:, 0, j * M:(j + 1) * M], xm))
            out_N(S["va"], full, meta=pT[0:M, 1, :])
            for j in range(4):
                out_T(S["qb"], j, xr)
            out_T(S["kb"], 0, xr, meta=(pO[:, 1, 0:M], xm))
            out_N(S["vb"], full, meta=pO[0:M, 0, 0:P])
            pe.wait_ge(tables_ready, 1)
            pe.wait_ge(evicted, S["vb"].o0 + NQ)
            attention(PH["diff"])
            attention(PH["win"])
            for n in range(KD):
                out_T(S[f"mrg_ga{n}"], 0, xr)
                out_T(S[f"mrg_gb{n}"], 0, xr)
                if n == 0:
                    pe.wait_ge(rhs_ready, PL.r["mrg"])
                out_T(S[f"mrg_a{n}"], 0, of(ya_))
                out_T(S[f"mrg_b{n}"], 0, of(yb_))
            for j in range(KD):
                out_T(S["wo"], j, of(mg), rhs_wait=None if j else PL.r["mrg"])
            out_T(S["ffgu"], 0, xr, rhs_wait=PL.r["x1"])
            norm_sum("x1")
            for j in range(1, 2 * KFF1):
                out_T(S["ffgu"], j, xr)
            for j in range(KD):
                out_T(S["ffd"], j, of(ffh), rhs_wait=None if j else PL.r["ff"])
            norm_sum("x2")
            out_T(S["cv"], 0, xr, rhs_wait=PL.r["xb"])
            norm_sum("xb", natural=True)
            for j in range(1, 12):
                out_T(S["cv"], j, xr)
            for j in range(6):
                out_T(S["cq"], j, xr)
            out_T(S["ckv"], 0, xr)
            norm_sum("cq")
            out_T(S["ckv"], 1, xr)
            out_T(S["kr"], 0, xr)

            def rope(n, o):
                pe.wait_ge(evicted, o + 1)
                if n:
                    pe.wait_ge(rope_done, n)
                pe.matmul(pT[:, 0, :], swap[:, :], qr[:, (2, 0, 1)[n], :], start=True, stop=True).then_inc(rope_mm, 1)

            pe.wait_ge(tables_ready, 1)
            for j in range(4):
                out_T(S["qn"], j, of(cqs), rhs_wait=None if j else PL.r["cq"])
            rope(0, S["kr"].o0)
            for j in range(2):
                out_T(S["qr"], j, of(cqs))
            out_T(S["kn"], 0, of(cks), rhs_wait=PL.r["ckv"])
            norm_sum("ckv", natural=True)
            for j in range(1, 4):
                out_T(S["kn"], j, of(cks))
            rope(1, S["qr"].o0)
            rope(2, S["qr"].o0 + 1)
            out_N(S["vm"], lambda q, k: cks[q][:, k, :])
            pe.wait_ge(rope_done, 3)
            pe.wait_ge(evicted, S["vm"].o0 + NQ)
            attention(PH["mla"])
            pe.wait_ge(rhs_ready, PL.r["p1"])
            for j in range(KD):
                out_T(S["awo"], j, of(mx))
            norm_sum("ma")

            def mlp(lay, p_in, h, m):
                out_T(S[f"up{lay}"], 0, xr, rhs_wait=PL.r[p_in])
                norm_sum(p_in)
                for j in range(1, KFF2):
                    out_T(S[f"up{lay}"], j, xr)
                for j in range(KD):
                    out_T(S[f"dn{lay}"], j, of(ffh), rhs_wait=None if j else PL.r[h])
                norm_sum(m)

            mlp(0, "p1", "h0", "mb")
            out_T(S["kc"], 0, xr, rhs_wait=PL.r["p2"])
            norm_sum("p2", natural=True)
            out_T(S["kc"], 1, xr)
            for name, n in (("vc", 2), ("q2", 8), ("ks", 2), ("kw", 2)):
                for j in range(n):
                    out_T(S[name], j, xr)
            out_N(S["vv"], full)
            out_N(S["gt"], full)
            pe.wait_ge(rhs_ready, PL.r["hid"])
            for c, name in enumerate(("ck1", "cv1")):
                s = S[name]
                bank_free(s.o0)
                ps = pS[:, s.o0 % 4, 0:2 * NCMP].rearrange("p (a n) -> p a n", a=2)
                bs = pO[:, c, 0:1]
                for k in range(CL):
                    tau = s.tile(0, k)
                    wh, wl = weights(tau)
                    rh, rl = (z[q][:, 2 * c:2 * c + 2, k:k + 16 * (NCMP - 1) + 1:16] for q in range(2))
                    bh, bl = (pe_s[q][:, c * CL + k:c * CL + k + 1] for q in range(2))
                    f, l = k == 0, k == CL - 1
                    pe.matmul(bs, wh, bh, start=f, stop=False)
                    pe.matmul(bs, wh, bl, start=False, stop=False)
                    pe.matmul(bs, wl, bh, start=False, stop=l)
                    pe.matmul(ps, wh, rh, start=f, stop=False)
                    pe.matmul(ps, wh, rl, start=False, stop=False)
                    mm = pe.matmul(ps, wl, rh, start=False, stop=l)
                    if (tau, 0) in PL.marks:
                        mm.then_inc(mm_done, 1)
            out_T(S["ck2"], 0, lambda q, k: hid[q][:, 0, 0:2 * NCMP], n_cols=2 * NCMP, rhs_wait=PL.r["hid"])
            s = S["cv2"]
            bank_free(s.o0)
            pe.wait_ge(rhs_ready, PL.r["hid"] + 2)
            wh, wl = weights(s.tau0)
            for a in range(2):
                ps = pS[0:NCMP, s.o0 % 4, a * P:(a + 1) * P]
                hh, hl = (hid[q][:, 1, a * NCMP:(a + 1) * NCMP] for q in range(2))
                pe.matmul(ps, hh, wh, start=True, stop=False)
                pe.matmul(ps, hl, wh, start=False, stop=False)
                mm = pe.matmul(ps, hh, wl, start=False, stop=True)
            mm.then_inc(mm_done, 1)
            pe.wait_ge(evicted, s.o0 + 1)
            attention(PH["nsa"])
            pe.wait_ge(rhs_ready, PL.r["p3"])
            for j in range(KD):
                out_T(S["cwo"], j, xr)
            norm_sum("mc")
            mlp(1, "p3", "h1", "md")

        @block.scalar
        def _(act):
            n_hi = [0]

            def split_hi(tau_last, look=LOOK):
                while n_hi[0] < min(tau_last // TPU + look + 1, PL.n_units):
                    u = n_hi[0]
                    act.wait_ge(raw_loaded[u % RAW], 16 * (u // RAW + 1))
                    if u >= WR:
                        act.wait_ge(mm_done, PL.unit_ms[u - WR])
                    act.activation(w_hi[:, u % WR, :], w_raw[:, u % RAW, :], ACT.Copy, scale=WS).then_inc(hi_split, 1)
                    n_hi[0] += 1

            def out_of(s, j=0):
                split_hi(PL.out_tau[s.o0 + j])

            def hi(r, dst, a, scale=1.0):
                act.activation(dst, a, ACT.Identity, scale=scale).then_inc(rhs_hi, 1)

            def square(q, a, n=T):
                if q >= 2:
                    act.wait_ge(sq_summed, q - 1)
                act.activation(sq[:, q % 2, 0:n], a, ACT.Square).then_inc(squared, 1)

            def norm_root(name, n, after_mm=True, meta=False, natural=False, rs_to=None, rn_to=None):
                act.wait_ge(norm_mm, NORM[name] + 1)
                f = WS * WS if after_mm else 1.0
                b = epsb[:, 0:1] if after_mm else epsb[:, 1:2]
                rs_to = rs if rs_to is None else rs_to
                rn_to = rn if rn_to is None else rn_to
                if meta:
                    act.activation(rs_to[:, T:TM], pO[:, 1, 8:8 + M], ACT.Sqrt, bias=b, scale=f / n)
                    act.activation(rn_to[0:M, NQ:NQ + 1], pO[0:M, 1, 4:5], ACT.Sqrt, bias=epsb[0:M, 0:1], scale=f / n)
                if natural:
                    act.activation(rn_to[:, 0:NQ], pO[:, 1, 0:NQ], ACT.Sqrt, bias=b, scale=f / n)
                act.activation(rs_to[:, 0:T], pT[:, 1, :], ACT.Sqrt, bias=b, scale=f / n).then_inc(norm_root_, 1)

            def probabilities(ph, t):
                act.wait_ge(maxed, t.t + 1)
                if t.t >= 3:
                    act.wait_ge(transposed, items_done(t.t - 3))
                G = (ph.g0 + t.group) % 4
                if t.kind == "cmp":
                    act.activation(p_sb[:, t.t % 3, 0:T], p_sb[:, t.t % 3, 0:T], ACT.Exp).then_inc(probs, 1)
                    return
                s_ = score_view(ph, t)
                act.activation(p_sb[:, t.t % 3, 0:s_.shape[1]], s_, ACT.Exp, bias=nmax[:, G, t.j:t.j + 1],
                               accum_out=sums[:, G, t.j:t.j + 1]).then_inc(probs, 1)

            def move_pt(ph, t):
                if pt_on_dve(t.t):
                    return
                act.wait_ge(transposed, t.item + 1)
                for d, s_ in p_parts(ph, t):
                    ins = act.activation(d, s_, ACT.Copy)
                ins.then_inc(pt_act, 1)

            def y_hi(ph, item, y, dst, scale):
                act.wait_ge(transposed, item + 1)
                d, s_ = y_parts(ph, y, dst[0], pT[:, item % 2, :])
                act.activation(d, s_, ACT.Identity, scale=scale).then_inc(rhs_hi, 1)

            def sink(g):
                act.wait_ge(tanh_in, 1 + g + 1)
                act.activation(sink_e[:, :], sink_e[:, :], ACT.Exp).then_inc(sink_exp, 1)

            def attention(ph, y_dst, y_scale, look_tau):
                split_hi(look_tau, 2)
                ts = ph.tasks
                for n, t in enumerate(ts):
                    if t.kind == "win" and n and t.j == 0:
                        sink(t.group - 1)
                    probabilities(ph, t)
                    if n:
                        move_pt(ph, ts[n - 1])
                        for item, y in ph.y_at.get(n - 1, []):
                            y_hi(ph, item, y, y_dst, y_scale)
                if t.kind == "win":
                    sink(t.group)
                move_pt(ph, t)
                for item, y in ph.y_at.get(n, []):
                    y_hi(ph, item, y, y_dst, y_scale)

            act.wait_ge(x_loaded, 16)
            act.wait_ge(par_loaded, 16)
            for k in range(KD):
                square(k, X[:, k, :], TM)
                hi(PL.r["x0"] + k, xa[0][:, k, :], X[:, k, :], pcol("g_mix", k))
                if k == 1:
                    split_hi(0, 1)
            act.wait_ge(basics_ready, 1)
            norm_root("x0", D, meta=True, natural=True)
            for name in ("qa", "ka", "va", "qb", "kb", "vb"):
                for j in range(S[name].n):
                    out_of(S[name], j)
            act.wait_ge(tanh_in, 1)
            act.activation(lam[:, 0:2], lam[:, 0:2], ACT.Exp).then_inc(act_out, 1)
            attention(PH["diff"], ya_, lam[:, 3:4], S["mrg_ga0"].tau0)
            attention(PH["win"], yb_, 1.0, S["mrg_ga0"].tau0)
            for n in range(KD):
                for c, name in enumerate(("ga", "gb")):
                    s = S[f"mrg_{name}{n}"]
                    out_of(s)
                    act.wait_ge(evicted, s.o0 + 1)
                    act.activation(tmp[:, c, :], tmp[:, c, :], ACT.Tanh, scale=0.5).then_inc(act_out, 1)
                out_of(S[f"mrg_a{n}"])
                out_of(S[f"mrg_b{n}"])
                act.wait_ge(computed, PL.s["mrg"] + n + 1)
                hi(PL.r["mrg"] + n, mg[0][:, n, :], src[:, n % 2, :], 0.5 / WS)
            for n in range(KD):
                out_of(S["wo"], n)
                act.wait_ge(evicted, S["wo"].o0 + n + 1)
                square(PL.q["x1"] + n, X[:, n, 0:T])
                hi(PL.r["x1"] + n, xa[0][:, n, 0:T], X[:, n, 0:T], pcol("g_ffn", n))
            out_of(S["ffgu"], 0)
            norm_root("x1", D)
            for n in range(KFF1):
                out_of(S["ffgu"], 2 * n)
                act.wait_ge(evicted, S["ffgu"].o0 + 2 * n + 1)
                act.activation(tmp[:, 1, :], tmp[:, 0, :], ACT.Tanh, scale=0.5).then_inc(act_out, 1)
                out_of(S["ffgu"], 2 * n + 1)
                act.wait_ge(computed, PL.s["ff"] + n + 1)
                hi(PL.r["ff"] + n, ffh[0][:, n, :], src[:, n % 2, :])
            for n in range(KD):
                out_of(S["ffd"], n)
                act.wait_ge(evicted, S["ffd"].o0 + n + 1)
                square(PL.q["x2"] + n, X[:, n, 0:T])
            norm_root("x2", D, after_mm=False)
            for n in range(KD):
                act.wait_ge(computed, PL.s["xb"] + n + 1)
                hi(PL.r["xb"] + n, xa[0][:, n, 0:T], X[:, n, 0:T], pcol("g_pre0", n))
                square(PL.q["xb"] + n, X[:, n, 0:T])
            out_of(S["cv"], 0)
            norm_root("xb", D, natural=True)
            for n in range(4):
                for j in range(3):
                    out_of(S["cv"], 3 * n + j)
                act.wait_ge(computed, PL.s["conv"] + n + 1)
                hi(PL.r["conv"] + n, mx[0][:, n, :], src[:, n % 2, :])
            for name, n_, dst in (("cq", 6, cqs), ("ckv", 2, cks)):
                for n in range(n_):
                    out_of(S[name], n)
                    act.wait_ge(evicted, S[name].o0 + n + 1)
                    square(PL.q[name] + n, src[:, n % 2, :])
                    hi(PL.r[name] + n, dst[0][:, n, :], src[:, n % 2, :], pcol("g_" + name, n))
                    if name == "ckv" and n == 0:
                        norm_root("cq", 768, rs_to=rsq)
            out_of(S["kr"], 0)
            for name in ("qn", "qr"):
                for j in range(S[name].n):
                    out_of(S[name], j)
            out_of(S["kn"], 0)
            act.wait_ge(evicted, S["kn"].o0)
            norm_root("ckv", 256, natural=True, rs_to=rsq, rn_to=rnk)
            for j in range(1, 4):
                out_of(S["kn"], j)
            out_of(S["vm"], 0)
            attention(PH["mla"], [mx[0][:, 4:8, :], mx[1][:, 4:8, :]], 1.0, S["awo"].tau0)

            def post_norm(s, m, g_in=None, p_name=None):
                for n in range(KD):
                    out_of(s, n)
                    act.wait_ge(evicted, s.o0 + n + 1)
                    square(PL.q[m] + n, m_view(m, n))
                norm_root(m, D, after_mm=False)
                if p_name is None:
                    return
                for n in range(KD):
                    act.wait_ge(computed, PL.s[p_name] + n + 1)
                    hi(PL.r[p_name] + n, xa[0][:, n, 0:T], X[:, n, 0:T], pcol(g_in, n))
                    square(PL.q[p_name] + n, X[:, n, 0:T])

            def mlp(lay, p_in, h):
                out_of(S[f"up{lay}"], 0)
                norm_root(p_in, D)
                for n in range(KFF2):
                    out_of(S[f"up{lay}"], n)
                    act.wait_ge(computed, PL.s[h] + n + 1)
                    hi(PL.r[h] + n, ffh[0][:, n, :], src[:, n % 2, :])

            post_norm(S["awo"], "ma", "g_mpre0", "p1")
            mlp(0, "p1", "h0")
            post_norm(S["dn0"], "mb", "g_pre1", "p2")
            out_of(S["kc"], 0)
            norm_root("p2", D, natural=True)
            for c, name in enumerate(("kc", "vc")):
                for j in range(2):
                    out_of(S[name], j)
                    act.wait_ge(evicted, S[name].o0 + j + 1)
                    hi(PL.r["z"] + 2 * c + j, z[0][:, 2 * c + j, :], src[:, j, :])
            hi(PL.r["pe"], pe_s[0], pcol("pe", 0, 64))
            for name in ("q2", "ks", "kw", "vv", "gt"):
                for j in range(S[name].n):
                    out_of(S[name], j)
            act.wait_ge(evicted, S["gt"].o0 + NQ)
            gf = gates.rearrange("p a b -> p (a b)")
            act.activation(gf, gf, ACT.Tanh, scale=0.5).then_inc(act_out, 1)
            for c, name in enumerate(("ck1", "cv1")):
                out_of(S[name], 0)
                act.wait_ge(tanh_in, 5 + c + 1)
                act.activation(tmp[:, 2, 0:2 * NCMP], tmp[:, 2, 0:2 * NCMP], ACT.Tanh,
                               scale=0.7978845608028654).then_inc(act_out, 1)
                act.wait_ge(computed, PL.s["hid"] + c + 1)
                hi(PL.r["hid"] + c, hid[0][:, c, 0:2 * NCMP], src[:, c, 0:2 * NCMP], 0.5)
            out_of(S["ck2"], 0)
            out_of(S["cv2"], 0)
            attention(PH["nsa"], xa, 1.0, S["cwo"].tau0)
            post_norm(S["cwo"], "mc", "g_mpre1", "p3")
            mlp(1, "p3", "h1")
            post_norm(S["dn1"], "md")

        @block.vector
        def _(dve):
            n_lo = [0]
            chain = [0]

            def link(ins):
                chain[0] += 1
                ins.then_inc(dve_chain, 1)

            def sync():
                dve.wait_ge(dve_chain, chain[0])

            def split_lo(tau_last, look=LOOK):
                while n_lo[0] < min(tau_last // TPU + look + 1, PL.n_units):
                    u = n_lo[0]
                    dve.wait_ge(hi_split, u + 1)
                    dve.scalar_tensor_tensor(out=w_lo[:, u % WR, :], in0=w_raw[:, u % RAW, :], scalar=WS,
                                             in1=w_hi[:, u % WR, :], op0=ALU.mult, op1=ALU.subtract).then_inc(lo_split, 1)
                    n_lo[0] += 1

            def out_of(s, j=0):
                o = s.o0 + j
                split_lo(PL.out_tau[o])
                dve.wait_ge(mm_done, PL.out_ms[o])
                return pS[:, o % 4, :]

            def lo(r, dst, a, h, scale=1.0):
                dve.wait_ge(rhs_hi, r + 1)
                dve.scalar_tensor_tensor(out=dst, in0=a, scalar=scale, in1=h, op0=ALU.mult,
                                         op1=ALU.subtract).then_inc(rhs_ready, 1)

            def add_square(name, k, n=T):
                q = PL.q[name] + k
                dve.wait_ge(squared, q + 1)
                if k == 0:
                    dve.tensor_copy(acc[:, 0:n], sq[:, q % 2, 0:n]).then_inc(sq_summed, 1)
                else:
                    dve.wait_ge(sq_summed, q)
                    dve.tensor_tensor(acc[:, 0:n], acc[:, 0:n], sq[:, q % 2, 0:n], ALU.add).then_inc(sq_summed, 1)

            def norm_recip(name, meta=False, natural=False, rs_to=None, rn_to=None):
                rs_to = rs if rs_to is None else rs_to
                rn_to = rn if rn_to is None else rn_to
                dve.wait_ge(norm_root_, NORM[name] + 1)
                n = TM if meta else T
                if meta:
                    link(dve.reciprocal(rn_to[0:M, NQ:NQ + 1], rn_to[0:M, NQ:NQ + 1]))
                if natural:
                    link(dve.reciprocal(rn_to[:, 0:NQ], rn_to[:, 0:NQ]))
                link(dve.reciprocal(rs_to[:, 0:n], rs_to[:, 0:n]))
                sync()

            def evict(s, j, dst, r=rs):
                ps = out_of(s, j)
                dve.tensor_tensor(dst, ps, r[:, 0:T], ALU.mult).then_inc(evicted, 1)

            def evict_scaled(s, j, dst, f, r=rs):
                ps = out_of(s, j)
                dve.scalar_tensor_tensor(out=dst, in0=ps, scalar=f, in1=r[:, 0:T], op0=ALU.mult,
                                         op1=ALU.mult).then_inc(evicted, 1)

            def evict_N(s, t, dst, w, rcol):
                ps = out_of(s, t)
                dve.tensor_scalar(dst, ps[:, 0:w], rcol, None, ALU.mult).then_inc(evicted, 1)

            def moved(s, j):
                dve.wait_ge(evicted, s.o0 + j + 1)

            def row_max(ph, t):
                dve.wait_ge(scores, t.t + 1)
                G = (ph.g0 + t.group) % 4
                s_ = score_view(ph, t)
                if t.kind == "cmp":
                    if t.t >= 3:
                        dve.wait_ge(transposed, items_done(t.t - 3))
                    a = p_sb[:, t.t % 3, 0:T]
                    a3 = a.rearrange("p (h n) -> p h n", h=16)
                    link(dve.tensor_tensor(a, s_, cbias[:, t.qi, :], ALU.add))
                    sync()
                    link(dve.tensor_reduce(cst[:, 0, :], a3, AX.X, ALU.max))
                    sync()
                    dve.tensor_tensor(a3, a3, cst[:, 0, :].unsqueeze(2).broadcast_to([P, 16, NCP]),
                                      ALU.subtract).then_inc(maxed, 1)
                    return
                nm = nmax[:, G, t.j:t.j + 1]
                if t.kind == "win":
                    link(dve.tensor_reduce(nm, s_, AX.X, ALU.max, negate=True))
                    sync()
                    dve.tensor_tensor(nm, nm, nsink[:, t.h:t.h + 1], ALU.min).then_inc(maxed, 1)
                    if t.last:
                        dve.wait_ge(maxed, t.t + 1)
                        dve.tensor_tensor(sink_e[:, :], pcol("sink", 0, 8), nmax[:, G, :], ALU.add).then_inc(tanh_in, 1)
                else:
                    dve.tensor_reduce(nm, s_, AX.X, ALU.max, negate=True).then_inc(maxed, 1)

            def move_pt(ph, t):
                if not pt_on_dve(t.t):
                    return
                dve.wait_ge(transposed, t.item + 1)
                for d, s_ in p_parts(ph, t):
                    ins = dve.tensor_copy(d, s_)
                ins.then_inc(pt_dve, 1)

            def bc(a, n, w):
                return a.unsqueeze(2).broadcast_to([P, n, w])

            def rows_free(ph, y):
                if y >= 4:
                    dve.wait_ge(transposed, y_item(ph, y - 4) + 1)

            def group_out(ph, g):
                G = ph.g0 + g
                b = pO[:, G % 2, :]
                s8 = sums[:, G % 4, :]
                c8 = scale8[:, G % 2, :]
                dve.wait_ge(av_done, G + 1)
                if ph.name == "diff":
                    link(dve.reciprocal(c8[:, 0:4], s8[:, 0:4]))
                    sync()
                    link(dve.tensor_tensor(c8[:, 0:4], c8[:, 0:4], sgn[:, :], ALU.mult))
                    sync()
                    t1 = tmp[:, 0, :]
                    dve.tensor_tensor(t1.rearrange("p (a e) -> p a e", a=4), b.rearrange("p (a e) -> p a e", a=4),
                                      bc(c8[:, 0:4], 4, P), ALU.mult).then_inc(grp_out, 1)
                    dve.wait_ge(grp_out, G + 1)
                    t4 = t1.rearrange("p (h s e) -> p h s e", h=2, s=2)
                    y = tmp[:, 1, 0:2 * P]
                    y3 = y.rearrange("p (h e) -> p h e", h=2)
                    link(dve.tensor_tensor(y3, t4[:, :, 0, :], t4[:, :, 1, :], ALU.add))
                    sync()
                    t2 = tmp[:, 2, 0:2 * P]
                    link(dve.tensor_tensor(t2, y, y, ALU.mult))
                    sync()
                    link(dve.tensor_reduce(ssq[:, g % 2, 4:6], t2.rearrange("p (h e) -> p h e", h=2), AX.X, ALU.add))
                    sync()
                    dve.tensor_scalar(ssq[:, g % 2, 0:2], ssq[:, g % 2, 4:6], 1.0 / P, EPS, ALU.mult, ALU.add).then_inc(pow_in, 1)
                    dve.wait_ge(pow_out, g + 1)
                    rows_free(ph, g)
                    dve.tensor_tensor(o_nat[:, g % 4, 0:2 * P].rearrange("p (h e) -> p h e", h=2), y3,
                                      bc(ssq[:, g % 2, 2:4], 2, P), ALU.mult).then_inc(y_done, 1)
                    return
                b3 = b.rearrange("p (h e) -> p h e", h=8)
                if ph.name == "win":
                    dve.wait_ge(sink_exp, g + 1)
                    link(dve.tensor_tensor(s8, s8, sink_e[:, :], ALU.add))
                    sync()
                if ph.name in ("win", "mla"):
                    link(dve.reciprocal(c8, s8))
                    sync()
                    rows_free(ph, g)
                    dve.tensor_tensor(o_nat[:, g % 4, :].rearrange("p (h e) -> p h e", h=8), b3, bc(c8, 8, HD),
                                      ALU.mult).then_inc(grp_out, 1)
                    return
                qi, k = g // 6, g % 6
                half, br = k % 2, k // 2
                if br == 0:
                    link(dve.reciprocal(c8, cst[:, 1, half * 8:half * 8 + 8]))
                    sync()
                    link(dve.tensor_scalar(c8, c8, has[:, qi:qi + 1], None, ALU.mult))
                else:
                    link(dve.reciprocal(c8, s8))
                sync()
                link(dve.tensor_tensor(c8, c8, gates[:, qi, br * 16 + half * 8:br * 16 + half * 8 + 8], ALU.mult))
                sync()
                y = 2 * qi + half
                rows = o_nat[:, y % 4, :]
                if br == 0:
                    rows_free(ph, y)
                    dve.tensor_tensor(rows.rearrange("p (h e) -> p h e", h=8), b3, bc(c8, 8, HD), ALU.mult).then_inc(grp_out, 1)
                    return
                t1 = tmp[:, k % 2, :]
                dve.tensor_tensor(t1.rearrange("p (h e) -> p h e", h=8), b3, bc(c8, 8, HD), ALU.mult).then_inc(grp_out, 1)
                dve.wait_ge(grp_out, G + 1)
                ins = dve.tensor_tensor(rows, rows, t1, ALU.add)
                if br == 1:
                    link(ins)
                    sync()
                else:
                    ins.then_inc(y_done, 1)

            def y_lo(ph, item, y, dst, scale):
                dve.wait_ge(rhs_hi, ITEMS[item][1] + 1)
                d, s_ = y_parts(ph, y, dst[1], pT[:, item % 2, :])
                h, _ = y_parts(ph, y, dst[0], pT[:, item % 2, :])
                dve.scalar_tensor_tensor(out=d, in0=s_, scalar=scale, in1=h, op0=ALU.mult,
                                         op1=ALU.subtract).then_inc(rhs_ready, 1)

            def attention(ph, y_dst, y_scale, look_tau):
                split_lo(look_tau, 2)
                ts = ph.tasks
                row_max(ph, ts[0])
                for n, t in enumerate(ts):
                    if n + 1 < len(ts):
                        row_max(ph, ts[n + 1])
                    if t.kind == "cmp":
                        dve.wait_ge(probs, t.t + 1)
                        link(dve.tensor_reduce(cst[:, 1, :], p_sb[:, t.t % 3, 0:T].rearrange("p (h n) -> p h n", h=16),
                                               AX.X, ALU.add))
                    move_pt(ph, t)
                    for g in group_ends(ph, n - 2):
                        group_out(ph, g)
                    if n == len(ts) - 1:
                        for g in group_ends(ph, n - 1) + group_ends(ph, n):
                            group_out(ph, g)
                    if n:
                        for item, y in ph.y_at.get(n - 1, []):
                            y_lo(ph, item, y, y_dst, y_scale)
                for item, y in ph.y_at.get(len(ts) - 1, []):
                    y_lo(ph, item, y, y_dst, y_scale)

            dve.memset(ones[:, :], 1.0)
            dve.memset(epsb[:, 0:1], EPS * WS * WS)
            dve.memset(epsb[:, 1:2], EPS)
            dve.memset(half_neg[:, :], -0.5).then_inc(basics_ready, 1)
            dve.wait_ge(par_loaded, 16)
            dve.wait_ge(x_loaded, 16)
            for k in range(KD):
                add_square("x0", k, TM)
                lo(PL.r["x0"] + k, xa[1][:, k, :], X[:, k, :], xa[0][:, k, :], pcol("g_mix", k))
                if k == 1:
                    split_lo(0, 1)
            norm_recip("x0", meta=True, natural=True)
            for j in range(4):
                evict_scaled(S["qa"], j, qa[:, j, :], 0.125)
            dve.wait_ge(const_loaded, 16)

            def table(name):
                a, b = CONST[name]
                return stage_c[:, a:b]

            dve.tensor_copy(ident[:, :], table("ident"))
            dve.tensor_copy(swap[:, :], table("swap"))
            dve.tensor_copy(identb[:, :], table("ident"))
            dve.tensor_copy(dist[:, :], table("dist"))
            dve.tensor_copy(band[:, :], table("band"))
            dve.tensor_copy(causal[:, :], table("causal"))
            dve.tensor_copy(aug[0:4, :, :].rearrange("p a b -> p (a b)"), table("aug")[0:4, :])
            dve.tensor_copy(rel[0:4, :], table("rel")[0:4, :])
            dve.tensor_copy(has[:, :], table("has"))
            for h in range(8):
                dve.tensor_scalar(sident[:, h, :], table("ident"), 2.0 ** -(h + 1), None, ALU.mult)
            link(dve.tensor_scalar(nsink[:, :], pcol("sink", 0, 8), -1.0, None, ALU.mult))
            dve.memset(sgn[:, :], 1.0).then_inc(tables_ready, 1)
            for j in range(4):
                if j == 3:
                    out_of(S["ka"], 3)
                    for h in range(4):
                        dve.tensor_tensor(ka[:, h, T:TM], pT[:, 0, h * M:(h + 1) * M], rs[:, T:TM], ALU.mult)
                evict(S["ka"], j, ka[:, j, 0:T])
            for t in range(NQ):
                out_of(S["va"], t)
                if t == 0:
                    dve.tensor_scalar(va[0:M, NQ, :], pT[0:M, 1, :], rn[0:M, NQ:NQ + 1], None, ALU.mult)
                evict_N(S["va"], t, va[:, t, :], T, rn[:, t:t + 1])
            for j in range(4):
                evict_scaled(S["qb"], j, qb[:, j, :], 0.125)
            out_of(S["kb"], 0)
            dve.tensor_tensor(kb_[:, T:TM], pO[:, 1, 0:M], rs[:, T:TM], ALU.mult)
            evict(S["kb"], 0, kb_[:, 0:T])
            for t in range(NQ):
                out_of(S["vb"], t)
                if t == 0:
                    dve.tensor_scalar(vb[0:M, NQ, :], pO[0:M, 0, 0:P], rn[0:M, NQ:NQ + 1], None, ALU.mult)
                evict_N(S["vb"], t, vb[:, t, :], P, rn[:, t:t + 1])
            lq = pcol("lam", 0, 256).rearrange("p (a b d) -> p a b d", a=2, b=2)
            t0 = tmp[:, 0, 0:P].rearrange("p (a d) -> p a d", a=2)
            link(dve.tensor_tensor(t0, lq[:, :, 0, :], lq[:, :, 1, :], ALU.mult))
            sync()
            dve.tensor_reduce(lam[:, 0:2], t0, AX.X, ALU.add).then_inc(tanh_in, 1)
            dve.wait_ge(act_out, 1)
            link(dve.tensor_tensor(lam[:, 2:3], lam[:, 1:2], lam[:, 0:1], ALU.subtract))
            link(dve.tensor_scalar(lam[:, 3:4], pcol("g_sub"), 1.0 - LINIT, None, ALU.mult))
            sync()
            for c in (1, 3):
                link(dve.tensor_scalar(sgn[:, c:c + 1], lam[:, 2:3], -LINIT, None, ALU.add))
            sync()
            attention(PH["diff"], ya_, lam[:, 3:4], S["mrg_ga0"].tau0)
            attention(PH["win"], yb_, 1.0, S["mrg_ga0"].tau0)
            for n in range(KD):
                for c, name in enumerate(("ga", "gb")):
                    evict(S[f"mrg_{name}{n}"], 0, tmp[:, c, :])
                for c, name in enumerate(("a", "b")):
                    s = S[f"mrg_{name}{n}"]
                    ps = out_of(s)
                    dve.wait_ge(act_out, 1 + 2 * n + c + 1)
                    dve.scalar_tensor_tensor(out=tmp[:, 2 + c, :], in0=tmp[:, c, :], scalar=1.0, in1=ps, op0=ALU.add,
                                             op1=ALU.mult).then_inc(evicted, 1)
                moved(s, 0)
                dve.tensor_tensor(src[:, n % 2, :], tmp[:, 2, :], tmp[:, 3, :], ALU.add).then_inc(computed, 1)
                lo(PL.r["mrg"] + n, mg[1][:, n, :], src[:, n % 2, :], mg[0][:, n, :], 0.5 / WS)

            def residual(s, n, f):
                ps = out_of(s, n)
                dve.scalar_tensor_tensor(out=X[:, n, 0:T], in0=ps, scalar=f, in1=X[:, n, 0:T], op0=ALU.mult,
                                         op1=ALU.add).then_inc(evicted, 1)

            for n in range(KD + 1):
                if n < KD:
                    residual(S["wo"], n, 1.0 / WS)
                if n:
                    add_square("x1", n - 1)
                    lo(PL.r["x1"] + n - 1, xa[1][:, n - 1, 0:T], X[:, n - 1, 0:T], xa[0][:, n - 1, 0:T], pcol("g_ffn", n - 1))
            norm_recip("x1")
            s = S["ffgu"]
            for n in range(KFF1):
                evict(s, 2 * n, tmp[:, 0, :])
                evict(s, 2 * n + 1, tmp[:, 2, :])
                dve.wait_ge(act_out, 17 + n + 1)
                link(dve.scalar_tensor_tensor(out=tmp[:, 3, :], in0=tmp[:, 1, :], scalar=1.0, in1=tmp[:, 0, :],
                                              op0=ALU.add, op1=ALU.mult))
                sync()
                dve.tensor_tensor(src[:, n % 2, :], tmp[:, 3, :], tmp[:, 2, :], ALU.mult).then_inc(computed, 1)
                lo(PL.r["ff"] + n, ffh[1][:, n, :], src[:, n % 2, :], ffh[0][:, n, :])
            for n in range(KD + 1):
                if n < KD:
                    residual(S["ffd"], n, 0.5 / WS)
                if n:
                    add_square("x2", n - 1)
            norm_recip("x2")
            for n in range(KD + 1):
                if n < KD:
                    dve.scalar_tensor_tensor(out=X[:, n, 0:T], in0=X[:, n, 0:T], scalar=pcol("g_fin", n),
                                             in1=rs[:, 0:T], op0=ALU.mult, op1=ALU.mult).then_inc(computed, 1)
                if n:
                    lo(PL.r["xb"] + n - 1, xa[1][:, n - 1, 0:T], X[:, n - 1, 0:T], xa[0][:, n - 1, 0:T], pcol("g_pre0", n - 1))
                    add_square("xb", n - 1)
            norm_recip("xb", natural=True)
            link(dve.memset(vpad[:, 0:2], 0.0))
            s = S["cv"]
            for n in range(4):
                evict(s, 3 * n, tmp[:, 0, :])
                evict(s, 3 * n + 1, tmp[:, 1, :])
                moved(s, 3 * n + 1)
                link(dve.tensor_tensor(vpad[:, 2:2 + T], tmp[:, 0, :], tmp[:, 1, :], ALU.mult))
                sync()
                link(dve.tensor_scalar(tmp[:, 2, :], vpad[:, 2:2 + T], pcol("conv", 3 * n + 2), None, ALU.mult))
                for c in (1, 0):
                    sync()
                    link(dve.scalar_tensor_tensor(out=tmp[:, 2, :], in0=vpad[:, c:c + T], scalar=pcol("conv", 3 * n + c),
                                                  in1=tmp[:, 2, :], op0=ALU.mult, op1=ALU.add))
                evict(s, 3 * n + 2, tmp[:, 0, :])
                sync()
                moved(s, 3 * n + 2)
                dve.tensor_tensor(src[:, n % 2, :], tmp[:, 2, :], tmp[:, 0, :], ALU.mult).then_inc(computed, 1)
                lo(PL.r["conv"] + n, mx[1][:, n, :], src[:, n % 2, :], mx[0][:, n, :])
            for name, n_, dst in (("cq", 6, cqs), ("ckv", 2, cks)):
                for n in range(n_):
                    evict(S[name], n, src[:, n % 2, :])
                    if name == "ckv" and n == 0:
                        dve.wait_ge(norm_mm, NORM["cq"] + 1)
                    add_square(name, n)
                    lo(PL.r[name] + n, dst[1][:, n, :], src[:, n % 2, :], dst[0][:, n, :], pcol("g_" + name, n))
                    if name == "ckv" and n == 0:
                        norm_recip("cq", rs_to=rsq)
            evict(S["kr"], 0, qr[:, 2, :])

            def rope(n):
                if n == 0:
                    dve.wait_ge(table_loaded, 32)
                a = qr[:, (2, 0, 1)[n], :]
                dve.wait_ge(rope_mm, n + 1)
                link(dve.tensor_tensor(tmp[:, 0, :], a, cos, ALU.mult))
                link(dve.tensor_tensor(tmp[:, 1, :], pT[:, 0, :], sin, ALU.mult))
                sync()
                dve.tensor_tensor(a, tmp[:, 0, :], tmp[:, 1, :], ALU.add).then_inc(rope_done, 1)

            for j in range(4):
                evict_scaled(S["qn"], j, qn[:, j, :], MLA_SCALE, rsq)
            rope(0)
            for j in range(2):
                evict_scaled(S["qr"], j, qr[:, j, :], MLA_SCALE, rsq)
            norm_recip("ckv", natural=True, rs_to=rsq, rn_to=rnk)
            for j in range(4):
                evict(S["kn"], j, kn[:, j, :], rsq)
            rope(1)
            rope(2)
            for t in range(NQ):
                evict_N(S["vm"], t, vm[:, t, :], T, rnk[:, t:t + 1])
            attention(PH["mla"], [mx[0][:, 4:8, :], mx[1][:, 4:8, :]], 1.0, S["awo"].tau0)

            def post_norm(s, m, g_post, next_, g_in=None):
                for n in range(KD + 1):
                    if n < KD:
                        ps = out_of(s, n)
                        dve.tensor_scalar(m_view(m, n), ps, 1.0 / WS, None, ALU.mult).then_inc(evicted, 1)
                    if n:
                        add_square(m, n - 1)
                norm_recip(m)
                for n in range(KD + 1):
                    if n < KD:
                        link(dve.scalar_tensor_tensor(out=tmp[:, n % 2, :], in0=m_view(m, n), scalar=pcol(g_post, n),
                                                      in1=rs[:, 0:T], op0=ALU.mult, op1=ALU.mult))
                        sync()
                        dve.tensor_tensor(X[:, n, 0:T], X[:, n, 0:T], tmp[:, n % 2, :], ALU.add).then_inc(computed, 1)
                    if n and g_in is not None:
                        lo(PL.r[next_] + n - 1, xa[1][:, n - 1, 0:T], X[:, n - 1, 0:T], xa[0][:, n - 1, 0:T], pcol(g_in, n - 1))
                        add_square(next_, n - 1)

            def mlp(lay, p_in, h, m):
                norm_recip(p_in)
                s = S[f"up{lay}"]
                for n in range(KFF2 + 1):
                    if n < KFF2:
                        evict(s, n, tmp[:, n % 2, :])
                        moved(s, n)
                        dve.scalar_tensor_tensor(out=src[:, n % 2, :], in0=tmp[:, n % 2, :], scalar=0.0,
                                                 in1=tmp[:, n % 2, :], op0=ALU.max, op1=ALU.mult).then_inc(computed, 1)
                    if n:
                        lo(PL.r[h] + n - 1, ffh[1][:, n - 1, :], src[:, (n - 1) % 2, :], ffh[0][:, n - 1, :])

            post_norm(S["awo"], "ma", "g_post0", "p1", "g_mpre0")
            mlp(0, "p1", "h0", "mb")
            post_norm(S["dn0"], "mb", "g_mpost0", "p2", "g_pre1")
            norm_recip("p2", natural=True)
            for c, name in enumerate(("kc", "vc")):
                for j in range(2):
                    evict(S[name], j, src[:, j, :])
                    lo(PL.r["z"] + 2 * c + j, z[1][:, 2 * c + j, :], src[:, j, :], z[0][:, 2 * c + j, :])
            lo(PL.r["pe"], pe_s[1], pcol("pe", 0, 64), pe_s[0])
            for j in range(8):
                evict_scaled(S["q2"], j, q2[:, j, :], 0.125)
            for j in range(2):
                evict(S["ks"], j, ks[:, j, :])
            for j in range(2):
                evict(S["kw"], j, kw[:, j, :])
            for t in range(NQ):
                evict_N(S["vv"], t, vv[:, t, :], T, rn[:, t:t + 1])
            for t in range(NQ):
                evict_N(S["gt"], t, gates[:, t, :], 48, rn[:, t:t + 1])
            dve.wait_ge(act_out, 40)
            gf = gates.rearrange("p a b -> p (a b)")
            link(dve.tensor_scalar(gf, gf, 0.5, 0.5, ALU.mult, ALU.add))
            link(dve.memset(kct, 0.0))
            link(dve.memset(vcbd, 0.0))
            nc2 = 2 * NCMP
            for c, name in enumerate(("ck1", "cv1")):
                ps = out_of(S[name], 0)
                link(dve.tensor_scalar(cst[:, 2, c:c + 1], pO[:, c, 0:1], 1.0 / WS, None, ALU.mult))
                sync()
                dve.tensor_scalar(tmp[:, 0, 0:nc2], ps[:, 0:nc2], 1.0 / WS, cst[:, 2, c:c + 1], ALU.mult,
                                  ALU.add).then_inc(evicted, 1)
                moved(S[name], 0)
                zz = tmp[:, 0, 0:nc2]
                t1 = tmp[:, 1, 0:nc2]
                link(dve.tensor_tensor(t1, zz, zz, ALU.mult))
                sync()
                link(dve.tensor_scalar(t1, t1, 0.044715, 1.0, ALU.mult, ALU.add))
                sync()
                dve.tensor_tensor(tmp[:, 2, 0:nc2], t1, zz, ALU.mult).then_inc(tanh_in, 1)
                dve.wait_ge(act_out, 41 + c)
                dve.scalar_tensor_tensor(out=src[:, c, 0:nc2], in0=tmp[:, 2, 0:nc2], scalar=1.0, in1=zz, op0=ALU.add,
                                         op1=ALU.mult).then_inc(computed, 1)
                lo(PL.r["hid"] + c, hid[1][:, c, 0:nc2], src[:, c, 0:nc2], hid[0][:, c, 0:nc2], 0.5)
            ps = out_of(S["ck2"], 0)
            for g in range(4):
                d = slice((g % 2) * HD, (g % 2 + 1) * HD)
                ins = dve.tensor_scalar(kct[d, g, 0:NCMP], ps[d, (g // 2) * NCMP:(g // 2 + 1) * NCMP], 1.0 / WS, None,
                                        ALU.mult)
            ins.then_inc(evicted, 1)
            ps = out_of(S["cv2"], 0)
            for r in range(4):
                ins = dve.tensor_scalar(vcbd[r * NCP:r * NCP + NCMP, :, r * HD:(r + 1) * HD],
                                        ps[0:NCMP, 0:256].rearrange("p (g d) -> p g d", g=4), 1.0 / WS, None, ALU.mult)
            ins.then_inc(evicted, 1)
            dve.wait_ge(table_loaded, 48)
            attention(PH["nsa"], xa, 1.0, S["cwo"].tau0)
            post_norm(S["cwo"], "mc", "g_post1", "p3", "g_mpre1")
            mlp(1, "p3", "h1", "md")
            post_norm(S["dn1"], "md", "g_mpost1", "out")

        @block.sync
        def _(sp):
            sp.dma_start(par[:, :], params).then_inc(par_loaded, 16)
            sp.dma_start(X[:, :, :], x_in).then_inc(x_loaded, 16)
            for u in range(RAW):
                sp.dma_start(w_raw[:, u, :], stream[u]).then_inc(raw_loaded[u], 16)
            sp.dma_start(stage_c, consts[:, 0:KEEP_TO]).then_inc(const_loaded, 16)

            def units(lo, hi):
                for u in range(lo, hi):
                    sp.wait_ge(lo_split, u - RAW + 1)
                    sp.dma_start(w_raw[:, u % RAW, :], stream[u]).then_inc(raw_loaded[u % RAW], 16)

            u1 = S["cq"].tau0 // TPU
            units(RAW, u1)
            sp.wait_ge(mm_done, PL.out_ms[S["cv"].o0 - 1])
            for name, v in (("cos", cos), ("sin", sin)):
                a, b = CONST[name]
                sp.dma_start(v, consts[:, a:b]).then_inc(table_loaded, 16)
            u2 = S["q2"].tau0 // TPU
            units(u1, u2)
            sp.wait_ge(mm_done, PL.out_ms[S["kc"].o0 - 1])
            a, b = CONST["cmpbias"]
            sp.dma_start(cbias.rearrange("p a b -> p (a b)"), consts[:, a:b]).then_inc(table_loaded, 16)
            units(u2, PL.n_units)
            for k in range(KD):
                sp.wait_ge(computed, PL.s["out"] + k + 1)
                sp.dma_start(out[:, k, :], X[:, k, 0:T]).then_inc(out_stored, 16)
            sp.wait_ge(out_stored, 16 * KD)

    return nc


def pack_stream(i):
    s = {}
    wi = i["w_in"][0]
    c = np.cumsum([0, 512, 512, 512, 512, 128, 128, 1024, 1024])
    s["qa"], s["ka"], s["va"], qb, s["kb"], s["vb"], ga, gb = (wi[:, c[n]:c[n + 1]] for n in range(8))
    s["qb"] = qb.reshape(D, 2, 4, HD).transpose(0, 2, 1, 3).reshape(D, 512)
    for n in range(KD):
        cols = slice(n * P, (n + 1) * P)
        s[f"mrg_ga{n}"], s[f"mrg_gb{n}"] = ga[:, cols], gb[:, cols]
        s[f"mrg_a{n}"], s[f"mrg_b{n}"] = i["w_branch_a"][0][:, cols], i["w_branch_b"][0][:, cols]
    s["wo"] = i["w_out"][0]
    s["ffgu"] = np.stack([i["w_ff_gate"][0].reshape(D, KFF1, P), i["w_ff_up"][0].reshape(D, KFF1, P)], 2).reshape(D, -1)
    s["ffd"] = i["w_ff_down"][0]
    a = i["a_w_in_2"][0]
    gb_, gc_, hv = (a[:, n * 512:(n + 1) * 512].reshape(D, 4, P) for n in range(3))
    s["cv"] = np.stack([gc_, hv, gb_], 2).reshape(D, -1)
    s["cq"], s["ckv"] = a[:, 1536:2304], a[:, 2304:2560]
    s["kr"] = np.tile(a[:, 2560:2592], (1, 4))
    q = i["a_w_q_up_2"][0].reshape(768, 8, 96)
    s["qn"], s["qr"] = q[:, :, :64].reshape(768, 512), q[:, :, 64:].reshape(768, 256)
    kv = i["a_w_kv_up_2"][0].reshape(256, 8, P)
    s["kn"], s["vm"] = kv[:, :, :64].reshape(256, 512), kv[:, :, 64:].reshape(256, 512)
    s["awo"] = i["a_w_out_2"][0]
    cw = i["c_w_in_2"][0]
    s["q2"] = cw[:, :1024].reshape(D, 2, 2, 4, HD).transpose(0, 1, 3, 2, 4).reshape(D, 1024)
    kc, vc, ks, vs, kw, vw = (cw[:, 1024 + 256 * n:1280 + 256 * n] for n in range(6))
    s["kc"], s["vc"], s["ks"], s["kw"] = kc, vc, ks, kw
    s["vv"] = np.concatenate([vs, vw], 1)
    s["gt"] = np.concatenate([cw[:, 2560:], np.zeros((D, 80), np.float32)], 1)

    def twice(w):
        b = np.zeros(w.shape[:-2] + (P, P), np.float32)
        b[..., :64, :64] = w
        b[..., 64:, 64:] = w
        return b.reshape(-1, P)

    s["ck1"], s["cv1"] = twice(i["c_cmp_w1_k_2"][0]), twice(i["c_cmp_w1_v_2"][0])
    s["ck2"], s["cv2"] = twice(i["c_cmp_w2_k_2"][0]), twice(i["c_cmp_w2_v_2"][0])
    s["cwo"] = i["c_w_out_2"][0]
    for lay in range(2):
        s[f"up{lay}"], s[f"dn{lay}"] = i["mlp_w1_2"][lay], i["mlp_w2_2"][lay]
    tiles = np.zeros((PL.n_units * TPU, P, P), np.float32)
    for st in PL.order:
        n = st.n if st.kind == "T" else st.width
        w = s[st.name].reshape(st.k, P, n, P)
        w = w.transpose(2, 0, 1, 3) if st.kind == "T" else w.transpose(0, 2, 1, 3)
        tiles[st.tau0:st.tau0 + n * st.k] = w.reshape(-1, P, P)
    return np.ascontiguousarray(tiles.reshape(PL.n_units, TPU, P, P).transpose(0, 2, 1, 3)).reshape(PL.n_units, P, UW)


def pack_params(i):
    def cols(g):
        return np.asarray(g, np.float32).reshape(-1, P).T

    def rows(g):
        return np.broadcast_to(np.asarray(g, np.float32).reshape(1, -1), (P, np.size(g)))

    def dup(pe):
        return np.concatenate([pe.T, pe.T], 0)

    parts = {"g_mix": cols(i["norm_mix"]), "g_ffn": cols(i["norm_ffn"]), "g_fin": cols(i["norm_final"]),
             "g_sub": cols(i["subln_gain"]), "g_cq": cols(i["a_q_norm_2"]), "g_ckv": cols(i["a_kv_norm_2"]),
             "conv": i["a_conv_w_2"][0].reshape(3, 4, P).transpose(2, 1, 0).reshape(P, 12),
             "sink": rows(i["sink_logits"]),
             "lam": rows(np.concatenate([i["lambda_q1"], i["lambda_k1"], i["lambda_q2"], i["lambda_k2"]], 0)),
             "pe": np.concatenate([dup(i["c_cmp_pe_k_2"][0]), dup(i["c_cmp_pe_v_2"][0])], 1)}
    for lay in range(2):
        parts[f"g_pre{lay}"], parts[f"g_post{lay}"] = cols(i["norm_mix_pre_2"][lay]), cols(i["norm_mix_post_2"][lay])
        parts[f"g_mpre{lay}"], parts[f"g_mpost{lay}"] = cols(i["norm_mlp_pre_2"][lay]), cols(i["norm_mlp_post_2"][lay])
    return np.ascontiguousarray(np.concatenate([parts[n] for n in PARAM], 1))


def kernel(**inputs):
    from concourse import bacc
    from concourse.bass_utils import run_bass_kernel_spmd

    i = {k: np.asarray(v) for k, v in inputs.items()}
    xt = np.concatenate([i["x"][0], i["meta_tokens"]], 0).T.reshape(KD, P, TM).transpose(1, 0, 2)
    arrays = {"in_x": np.ascontiguousarray(xt), "in_w": pack_stream(i), "in_c": CONSTANTS, "in_p": pack_params(i)}
    nc = bacc.Bacc("TRN2", target_bir_lowering=False, num_devices=1)
    args = [nc.dram_tensor(n, a.shape, F32, kind="ExternalInput").ap() for n, a in arrays.items()]
    args.append(nc.dram_tensor("out_t", (P, KD, T), F32, kind="ExternalOutput").ap())
    build_program(nc, *args)
    r = run_bass_kernel_spmd(nc, [arrays], core_ids=[0])
    y = r.results[0]["out_t"]
    return np.ascontiguousarray(y.transpose(2, 1, 0).reshape(1, T, D))
```

```python
from contextlib import ExitStack

import numpy as np

import concourse.bass as bass
from concourse import mybir
from concourse.alu_op_type import AluOpType as ALU

ACT = mybir.ActivationFunctionType
AX = mybir.AxisListType
F32 = mybir.dt.float32
F16 = mybir.dt.float16
BF16 = mybir.dt.bfloat16

P = 128
T = 512
NQ = T // P
M = 16
TM = T + M
D = 1024
KD = D // P
HD = 64
FF1 = 2816
KFF1 = FF1 // P
FF2 = 4096
KFF2 = FF2 // P
EPS = 1e-6
WS = 64.0
NEG = -1e30
NCMP = 31
NCP = 32
CL = 32
LINIT = 0.2
MLA_SCALE = 96.0 ** -0.5

TPU = 8
UW = TPU * P
RAW = 6
WR = 8
LOOK = 4


LEAD = 4
LEADS = ("qa", "ffgu", "cv", "up0", "kvc", "up1")


class Stage:

    def __init__(self, name, kind, n, k, width, o0, tau0):
        self.name, self.kind, self.n, self.k, self.width, self.o0, self.tau0 = name, kind, n, k, width, o0, tau0

    def tile(self, j, k):
        if self.name in LEADS and j < LEAD:
            return self.tau0 + k * LEAD + j
        return self.tau0 + (j * self.k + k if self.kind == "T" else k * self.width)


class Plan:

    def __init__(self):
        self.st, self.order = {}, []
        self.o = self.tau = self.ms = 0
        self.out_ms, self.unit_ms, self.out_tau, self.marks = [], {}, [], set()
        for name, kind, n, k, width in STAGES:
            if kind == "N":
                self.tau += (-self.tau) % width
            s = Stage(name, kind, n, k, width, self.o, self.tau)
            self.st[name] = s
            self.order.append(s)
            if kind == "T":
                if name in LEADS:
                    for kk in range(k):
                        for j in range(LEAD):
                            self.step(self.tau, 1, kk == k - 1)
                for j in range(LEAD if name in LEADS else 0, n):
                    for kk in range(k):
                        self.step(self.tau, 1, kk == k - 1)
            else:
                for t in range(n):
                    for kk in range(k):
                        tau = self.tau + kk * width
                        last = kk == k - 1
                        ends = t == n - 1 and (tau + width) % TPU == 0
                        if last or ends:
                            self.ms += 1
                            self.marks.add((tau, t))
                        if last:
                            self.out_ms.append(self.ms)
                            self.out_tau.append(tau + width - 1)
                        if ends:
                            self.unit_ms[tau // TPU] = self.ms
                self.tau += k * width
                self.o += n
        self.n_units = -(-self.tau // TPU)
        self.r = {}
        at = 0
        for name, n in RHS:
            self.r[name] = at
            at += n
        self.s = {}
        at = 0
        for name, n in SRC:
            self.s[name] = at
            at += n
        self.q = {}
        at = 0
        for name, n in SQUARES:
            self.q[name] = at
            at += n

    def step(self, tau, width, last):
        ends = (tau + width) % TPU == 0
        if last or ends:
            self.ms += 1
            self.marks.add((tau, 0))
        if last:
            self.out_ms.append(self.ms)
            self.out_tau.append(tau)
            self.o += 1
        if ends:
            self.unit_ms[tau // TPU] = self.ms
        self.tau += width


STAGES = (
    [("qa", "T", 4, KD, 1), ("ka", "T", 4, KD, 1), ("va", "N", NQ, KD, 4), ("qb", "T", 4, KD, 1),
     ("kb", "T", 1, KD, 1), ("vb", "N", NQ, KD, 1)]
    + [x for n in range(KD) for x in ((f"mrg_ga{n}", "T", 1, KD, 1), (f"mrg_gb{n}", "T", 1, KD, 1),
                                      (f"mrg_a{n}", "T", 1, 4, 1), (f"mrg_b{n}", "T", 1, 4, 1))]
    + [("wo", "T", KD, KD, 1), ("ffgu", "T", 2 * KFF1, KD, 1), ("ffd", "T", KD, KFF1, 1),
       ("cv", "T", 12, KD, 1), ("cq", "T", 6, KD, 1), ("ckv", "T", 2, KD, 1), ("kr", "T", 1, KD, 1),
       ("qn", "T", 4, 6, 1), ("qr", "T", 2, 6, 1), ("kn", "T", 4, 2, 1), ("vm", "N", NQ, 2, 4),
       ("awo", "T", KD, KD, 1), ("up0", "T", KFF2, KD, 1), ("dn0", "T", KD, KFF2, 1),
       ("kvc", "T", 4, KD, 1), ("ks", "T", 2, KD, 1), ("ck1", "T", 1, CL, 1), ("cv1", "T", 1, CL, 1),
       ("q2", "T", 8, KD, 1), ("kw", "T", 2, KD, 1), ("vv", "N", NQ, KD, 4),
       ("ck2", "T", 1, 1, 1), ("cv2", "T", 1, 1, 1), ("gt", "N", NQ, KD, 1),
       ("cwo", "T", KD, KD, 1), ("up1", "T", KFF2, KD, 1), ("dn1", "T", KD, KFF2, 1)]
)
RHS = [("x0", 8), ("qa", 4), ("ka", 4), ("va", 4), ("qb", 4), ("kb", 1), ("vb", 4), ("ya", 8), ("yb", 4), ("mrg", 8), ("x1", 8), ("ff", KFF1), ("xb", 8), ("conv", 4),
       ("cq", 6), ("ckv", 2), ("qn", 4), ("kr", 1), ("kn", 4), ("qr", 2), ("vm", 4), ("ymla", 4), ("p1", 8), ("h0", KFF2), ("p2", 8), ("z", 4), ("pe", 1),
       ("ks", 2), ("hid", 2), ("q2", 8), ("kw", 2), ("vv", 4), ("ynsa", 8), ("p3", 8), ("h1", KFF2)]
SRC = [("mrg", 8), ("ff", KFF1), ("xb", 8), ("conv", 4), ("p1", 8), ("h0", KFF2), ("p2", 8), ("hid", 2),
       ("p3", 8), ("h1", KFF2), ("out", 8)]
SQUARES = [("x0", 8), ("x1", 8), ("x2", 8), ("xb", 8), ("cq", 6), ("ckv", 2), ("ma", 8), ("p1", 8),
           ("mb", 8), ("p2", 8), ("mc", 8), ("p3", 8), ("md", 8)]
NORM = {n: i for i, (n, _) in enumerate(SQUARES)}
PL = Plan()


class Task:

    def __init__(self, kind, qi, h, kb, group, col, dv, j, last, s=0, b=0):
        self.kind, self.qi, self.h = kind, qi, h
        self.s, self.b = s, b
        self.kb = kb
        self.group, self.j, self.last = group, j, last
        self.col, self.dv = col, dv


class Phase:

    def __init__(self, name, tasks, t0, g0, i0, r0, y_after, slots):
        self.name, self.tasks, self.t0, self.g0, self.slots = name, tasks, t0, g0, slots
        self.ahead = min(slots, 3)
        self.lag = 1 if slots == 2 else 2
        self.items = []
        ny = 0
        self.y_at = {}
        for n, t in enumerate(tasks):
            t.n, t.t = n, t0 + n
            t.item = i0 + len(self.items)
            self.items.append(("P", t.t))
            for y, after in y_after:
                if n == min(after + 5, len(tasks) - 1):
                    self.y_at.setdefault(n, []).append((i0 + len(self.items), y))
                    self.items.append(("Y", r0 + y))
        self.n_groups = tasks[-1].group + 1
        self.t1, self.g1, self.i1 = t0 + len(tasks), g0 + self.n_groups, i0 + len(self.items)


def key_blocks(i):
    return list(range(max(0, i - 1), min(NQ, i + 2)))


def make_phases():
    out, t, g, i = {}, 0, 0, 0
    diff = []
    for qi in range(NQ):
        for h in range(4):
            for s in range(2):
                diff.append(Task(kind="diff", qi=qi, h=h, s=s, kb=list(range(NQ)), group=qi * 2 + h // 2,
                                 col=((h % 2) * 2 + s) * P, dv=P, j=(h % 2) * 2 + s, last=(h % 2 == 1 and s == 1)))
    y = [(k, 4 * k + 3) for k in range(8)]
    out["diff"] = p = Phase("diff", diff, t, g, i, PL.r["ya"], y, 2)
    t, g, i = p.t1, p.g1, p.i1
    for name, r in (("win", "yb"), ("mla", "ymla")):
        tasks = []
        for qi in range(NQ):
            for h in range(8):
                kb = key_blocks(qi) if name == "win" else list(range(qi + 1))
                tasks.append(Task(kind=name, qi=qi, h=h, kb=kb, group=qi, col=h * HD, dv=HD, j=h, last=h == 7))
        y = [(k, 8 * k + 7) for k in range(4)]
        out[name] = p = Phase(name, tasks, t, g, i, PL.r[r], y, 4)
        t, g, i = p.t1, p.g1, p.i1
    tasks, y = [], []
    for qi in range(NQ):
        tasks.append(Task(kind="cmp", qi=qi, h=0, kb=[0, 1, 2, 3], group=qi * 6 + 1, col=0, dv=HD, j=0, last=True))
        for b in range(2):
            for h in range(16):
                tasks.append(Task(kind="nsa", b=b, qi=qi, h=h, kb=list(range(qi + 1)), group=qi * 6 + 2 + b * 2 + h // 8,
                                  col=(h % 8) * HD, dv=HD, j=h % 8, last=h % 8 == 7))
                if b and h % 8 == 7:
                    y.append((qi * 2 + h // 8, len(tasks) - 1))
    out["nsa"] = Phase("nsa", tasks, t, g, i, PL.r["ynsa"], y, 4)
    return out


PH = make_phases()
ITEMS = [x for p in PH.values() for x in p.items]


def slopes(n):
    return (2.0 ** (-8.0 * np.arange(1, n + 1) / n)).astype(np.float32)


CONST = {}


def const_columns():
    p = np.arange(P)
    c = np.arange(896)
    parts = []

    def put(name, a):
        a = np.asarray(a, np.float32).reshape(P, -1)
        at = sum(x.shape[1] for x in parts)
        CONST[name] = (at, at + a.shape[1])
        parts.append(a)

    put("ident", np.eye(P))
    swap = np.zeros((P, P))
    for m in range(P):
        if m % 32 < 16:
            swap[m + 16, m] = -1
        else:
            swap[m - 16, m] = 1
    put("swap", swap)
    dist = p[:, None] + 384 - c[None, :]
    put("dist", -np.abs(dist))
    put("band", np.where(np.abs(dist) > 128, NEG, 0.0))
    put("causal", np.where(p[None, :] > p[:, None], NEG, 0.0))
    sl = slopes(16).astype(np.float64) * 64
    pieces = []
    for _ in range(3):
        h = sl.astype(np.float16).astype(np.float64)
        pieces.append(h)
        sl = sl - h
    aug = np.zeros((P, 16, P))
    for k in range(3):
        aug[k] = pieces[k][:, None]
    put("aug", aug)
    rel = np.zeros((P, 896))
    rel[:3] = (c - 384) / 64.0
    put("rel", rel)
    put("has", (p[:, None] + P * np.arange(NQ)[None, :] >= CL - 1).astype(np.float32))
    half = 16
    inv = (np.float32(10000.0) ** (-np.arange(half, dtype=np.float32) / np.float32(half))).astype(np.float32)
    ang = np.arange(T, dtype=np.float32)[None, :] * inv[p % 16][:, None]
    put("cos", np.cos(ang))
    put("sin", np.sin(ang))
    starts = np.arange(NCMP) * 16
    centre = starts + (CL - 1) / 2.0
    bias = np.full((P, NQ, 16, NCP), NEG, np.float32)
    for i in range(NQ):
        t = p + P * i
        for h in range(16):
            v = -slopes(16)[h] * (t[:, None] - centre[None, :]).astype(np.float32)
            ok = (starts + CL - 1)[None, :] <= t[:, None]
            bias[:, i, h, :NCMP] = np.where(ok, v, NEG)
    put("cmpbias", bias)
    return np.ascontiguousarray(np.concatenate(parts, axis=1))


CONSTANTS = const_columns()
KEEP_TO = CONST["has"][1]

PARAM, _at = {}, 0
for _name, _n in (("g_mix", 8), ("g_ffn", 8), ("g_fin", 8), ("g_pre0", 8), ("g_post0", 8), ("g_mpre0", 8),
                  ("g_mpost0", 8), ("g_pre1", 8), ("g_post1", 8), ("g_mpre1", 8), ("g_mpost1", 8),
                  ("g_sub", 1), ("g_cq", 6), ("g_ckv", 2), ("conv", 12), ("sink", 8), ("lam", 256),
                  ("pe", 64)):
    PARAM[_name] = (_at, _at + _n)
    _at += _n
N_PARAM = _at


def splits(s, j):
    return 1 if s.name in LEADS and j < LEAD else s.k // TPU + 1


def y_parts(ph, y, dst, ps):
    if ph.name in ("diff", "nsa"):
        qi, half = y // 2, y % 2
        n = 2 if ph.name == "diff" else 4
        k = half * n
    else:
        qi, k, n = y, 0, 4
    return (dst[:, k:k + n, qi * P:(qi + 1) * P], ps[:, 0:n * P].rearrange("p (a b) -> p a b", a=n))


def group_ends(ph, n):
    if n < 0 or not ph.tasks[n].last:
        return []
    g = ph.tasks[n].group
    return [g - 1, g] if ph.tasks[n].kind == "cmp" else [g]


def items_done(t):
    for ph in PH.values():
        if ph.t0 <= t < ph.t1:
            return ph.tasks[t - ph.t0].item + 1
    raise ValueError(t)


def n_added(g):
    return g // 6 * 4 + max(0, g % 6 - 2)


def y_item(ph, y):
    return [i for n in sorted(ph.y_at) for i, yy in ph.y_at[n] if yy == y][0]


def build_program(nc, x_in, stream, consts, params, out):
    ctx = ExitStack()
    with ctx:
        def sb(name, shape, dt=F32):
            return ctx.enter_context(nc.sbuf_tensor(name, shape, dt))

        def sem(name):
            return ctx.enter_context(nc.semaphore(name))

        w_raw = sb("w_raw", [P, RAW, UW])
        w_hi = sb("w_hi", [P, WR, UW], F16)
        w_lo = sb("w_lo", [P, WR, UW], F16)
        X = sb("X", [P, KD, TM])
        xx = sb("xx", [P, KD, 2, TM], F16)
        xx32 = xx[:, :, :, :].rearrange("p a b c -> p (a b c)").bitcast(F32).rearrange("p (a b) -> p a b", a=KD)
        xa = [xx[:, :, 0, :], xx[:, :, 1, :]]
        sq = sb("sq", [P, 2, TM])
        acc = sb("acc", [P, TM])
        rs = sb("rs", [P, TM])
        rn = sb("rn", [P, NQ + 1])
        rt = sb("rt", [P, 2, NQ + 1])
        diag = sb("diag", [P, TM])
        rsq = sb("rsq", [P, T])
        rnk = sb("rnk", [P, NQ])
        tmp = sb("tmp", [P, 4, T])
        src = sb("src", [P, 2, T])
        ident = sb("ident", [P, P])
        swap = sb("swap", [P, P])
        identh = sb("identh", [P, P], F16)
        identb = sb("identb", [P, P], BF16)
        sident = sb("sident", [P, 8, P], F16)
        dist = sb("dist", [P, 896], F16)
        band = sb("band", [P, 896], BF16)
        causal = sb("causal", [P, P], BF16)
        aug = sb("aug", [P, 16, P], F16)
        rel = sb("rel", [P, 896], F16)
        has = sb("has", [P, NQ])
        ones = sb("ones", [P, P])
        half_neg = sb("half_neg", [P, NQ + 1])
        par = sb("par", [P, N_PARAM])
        lam = sb("lam", [P, 4])
        nsink = sb("nsink", [P, 8])
        nmax = sb("nmax", [P, 4, 8])
        sums = sb("sums", [P, 4, 8])
        scale8 = sb("scale8", [P, 2, 8])
        sgn = sb("sgn", [P, 4])
        ssq = sb("ssq", [P, 2, 6])
        sink_e = sb("sink_e", [P, 8])
        cst = sb("cst", [P, 3, 16])
        ARENA = 19904
        arena = sb("arena", [P, ARENA])
        ar16 = arena[:, :].bitcast(F16)

        def view(at, shape, dt=F32):
            n = int(np.prod(shape))
            cols = n if dt == F32 else (n + 1) // 2
            assert at + cols <= ARENA, (at, shape)
            v = arena[:, at:at + n] if dt == F32 else ar16[:, 2 * at:2 * at + n]
            if len(shape) == 2:
                v = v.rearrange("p (a b) -> p a b", a=shape[0])
            if len(shape) == 3:
                v = v.rearrange("p (a b c) -> p a b c", a=shape[0], b=shape[1])
            return v, at + cols

        def pair(at, shape):
            h, at = view(at, shape, F16)
            l, at = view(at, shape, F16)
            return [h, l], at

        p_sb, at = view(0, [2, TM])
        p_hl, at = view(at, [4, TM], F16)
        pt_sb, at = view(at, [6, 5 * P], F16)
        o_nat, att0 = view(at, [4, T])
        qa, at = pair(att0, [4, T])
        ka, at = pair(at, [4, TM])
        va, at = pair(at, [NQ + 1, T])
        qb, at = pair(at, [4, T])
        kb_, at = pair(at, [TM])
        vb, at = pair(at, [NQ + 1, P])
        ya_, at = pair(at, [4, T])
        yb_, _ = pair(att0, [4, T])
        mg, at = pair(0, [KD, T])
        ffh, at = pair(0, [KFF2, T])
        stage_c, _ = view(ARENA - KEEP_TO, [KEEP_TO])
        cos, at = view(att0, [T])
        sin, at = view(at, [T])
        mx, at = pair(at, [KD, T])
        cq0 = at
        cqs, at = pair(at, [6, T])
        vm, _ = pair(cq0, [NQ, T])
        cks, at = pair(at, [2, T])
        vpad, _ = view(at, [2 + T])
        qr = o_nat
        qn, at = pair(at, [4, T])
        kn, at = pair(at, [4, T])
        krp, at = pair(at, [T])
        qrp, _ = pair(cq0 + 4 * T, [2, T])
        q2, at = pair(att0, [8, T])
        m_att, _ = view(att0, [8, T])
        ks, at = pair(at, [2, T])
        kw, at = pair(at, [2, T])
        vv, at = pair(at, [NQ, T])
        gates, at = view(at, [NQ, 48])
        kct, at = pair(at, [4, NCP])
        vcbd, at = pair(at, [4, 4 * HD])
        cbias, at = view(at, [NQ, T])
        z, at = pair(at, [4, T])
        pe_s, at = pair(at, [64])
        hid, at = pair(at, [2, 64])

        pS = ctx.enter_context(nc.psum_tensor("pS", [P, 4, 512], F32))
        pT = ctx.enter_context(nc.psum_tensor("pT", [P, 2, 512], F32))
        pO = ctx.enter_context(nc.psum_tensor("pO", [P, 2, 512], F32))

        x_loaded = sem("x_loaded")
        par_loaded = sem("par_loaded")
        const_loaded = sem("const_loaded")
        table_loaded = sem("table_loaded")
        raw_loaded = [sem(f"raw_loaded{i}") for i in range(RAW)]
        basics_ready = sem("basics_ready")
        tables_ready = sem("tables_ready")
        hi_split = sem("hi_split")
        lo_split = sem("lo_split")
        mm_done = sem("mm_done")
        evicted = sem("evicted")
        computed = sem("computed")
        rhs_hi = sem("rhs_hi")
        rhs_ready = sem("rhs_ready")
        squared = sem("squared")
        sq_summed = sem("sq_summed")
        norm_mm = sem("norm_mm")
        mean_ready = sem("mean_ready")
        rstd_ready = sem("rstd_ready")
        diag_ready = sem("diag_ready")
        norm_wide = sem("norm_wide")
        rs_ready = sem("rs_ready")
        dve_chain = sem("dve_chain")
        tanh_in = sem("tanh_in")
        act_out = sem("act_out")
        scores = sem("scores")
        maxed = sem("maxed")
        probs = sem("probs")
        probs_split = sem("probs_split")
        transposed = sem("transposed")
        pt_moved = sem("pt_moved")
        av_done = sem("av_done")
        grp_out = sem("grp_out")
        y_done = sem("y_done")
        sink_exp = sem("sink_exp")
        pool_added = sem("pool_added")
        rows_sq = sem("rows_sq")
        pool_chain = sem("pool_chain")
        rope_mm = sem("rope_mm")
        rope_done = sem("rope_done")
        out_stored = sem("out_stored")

        S = PL.st

        def pcol(name, k=0, n=1):
            a = PARAM[name][0]
            return par[:, a + k:a + k + n]

        def pt_psum(item):
            return pT[:, item % 2, :].bitcast(F16).rearrange("p (a b c) -> p a b c", a=2, b=4)

        def meta_psum(t):
            if t.kind == "diff":
                return pS[0:M, (t.t % 2) * 2 + 1, P:2 * P].bitcast(F16).rearrange("p (a b) -> p a b", a=2)
            return pt_psum(t.item)[0:M, :, 3, :]

        def pt_of(t):
            a = (t % 3) * 2
            return pt_sb[:, a:a + 2, :].rearrange("p a (b c) -> p a b c", b=5)

        def m_view(m, n):
            return m_att[:, n, :] if m == "mc" else xx32[:, n, 0:T]

        def score_view(ph, t):
            w = 4 // ph.slots
            sl = (t.t % ph.slots) * w
            if t.kind == "diff":
                return pS[:, sl:sl + 2, :].rearrange("p a b -> p (a b)")[:, 0:TM]
            if t.kind == "cmp":
                return pS[:, sl, :]
            return pS[:, sl, 0:len(t.kb) * P + (M if t.kind == "win" else 0)]

        block = ctx.enter_context(nc.Block())

        @block.gpsimd
        def _(pool):
            pool.wait_ge(basics_ready, 1)

            def norm_power(name, meta=False):
                pool.wait_ge(mean_ready, NORM[name] + 1)
                if meta:
                    pool.tensor_tensor(rt[0:M, 1, NQ:NQ + 1], rt[0:M, 0, NQ:NQ + 1], half_neg[0:M, 0:1], ALU.pow)
                pool.tensor_tensor(rt[:, 1, 0:NQ], rt[:, 0, 0:NQ], half_neg[:, 0:NQ], ALU.pow).then_inc(rstd_ready, 1)

            norm_power("x0", meta=True)
            pc = [0]

            def link(ins):
                pc[0] += 1
                ins.then_inc(pool_chain, 1)

            def bc(a, n, w):
                return a.unsqueeze(2).broadcast_to([P, n, w])

            def rows_free(ph, y):
                if y >= 4:
                    pool.wait_ge(transposed, y_item(ph, y - 4) + 1)

            for g in range(PH["diff"].n_groups):
                ph = PH["diff"]
                pool.wait_ge(grp_out, g + 1)
                t4 = tmp[:, g % 2, :].rearrange("p (h s e) -> p h s e", h=2, s=2)
                y3 = tmp[:, 2 + g % 2, 0:2 * P].rearrange("p (h e) -> p h e", h=2)
                pool.tensor_tensor(y3, t4[:, :, 0, :], t4[:, :, 1, :], ALU.add).then_inc(pool_added, 1)
                pool.wait_ge(rows_sq, g + 1)
                link(pool.tensor_scalar(ssq[:, g % 2, 2:4], ssq[:, g % 2, 0:2], 1.0 / P, EPS, ALU.mult, ALU.add))
                pool.wait_ge(pool_chain, pc[0])
                link(pool.tensor_tensor(ssq[:, g % 2, 4:6], ssq[:, g % 2, 2:4], half_neg[:, 0:2], ALU.pow))
                pool.wait_ge(pool_chain, pc[0])
                rows_free(ph, g)
                pool.tensor_tensor(o_nat[:, g % 4, 0:2 * P].rearrange("p (h e) -> p h e", h=2), y3,
                                   bc(ssq[:, g % 2, 4:6], 2, P), ALU.mult).then_inc(y_done, 1)
            norm_power("x1")
            norm_power("x2")
            norm_power("xb")
            norm_power("cq")
            norm_power("ckv")
            norm_power("ma")
            norm_power("p1")
            norm_power("mb")
            norm_power("p2")
            for g in range(PH["nsa"].n_groups):
                qi, k = g // 6, g % 6
                if k >= 2:
                    pool.wait_ge(grp_out, PH["nsa"].g0 + g + 1)
                    i = PH["diff"].n_groups + n_added(g)
                    pool.wait_ge(pool_added, i)
                    rows = o_nat[:, (2 * qi + k % 2) % 4, :]
                    pool.tensor_tensor(rows, rows, tmp[:, k % 2, :], ALU.add).then_inc(pool_added, 1)
            norm_power("mc")
            norm_power("p3")
            norm_power("md")

        @block.tensor
        def _(pe):
            unit = [-1]

            def weights(tau, n=1):
                u = tau // TPU
                if u != unit[0]:
                    pe.wait_ge(lo_split, u + 1)
                    unit[0] = u
                a = (tau % TPU) * P
                return w_hi[:, u % WR, a:a + n * P], w_lo[:, u % WR, a:a + n * P]

            def bank_free(o):
                if o >= 4:
                    pe.wait_ge(evicted, o - 3)

            def out_T(s, j, rhs, n_cols=T, meta=None, rhs_wait=None):
                o = s.o0 + j
                bank_free(o)
                ps = pS[:, o % 4, 0:n_cols]
                for k in range(s.k):
                    if rhs_wait is not None:
                        pe.wait_ge(rhs_ready, rhs_wait + k + 1)
                    tau = s.tile(j, k)
                    wh, wl = weights(tau)
                    ah, al = rhs(0, k), rhs(1, k)
                    f, l = k == 0, k == s.k - 1
                    if meta is not None:
                        mps, mr = meta
                        pe.matmul(mps, wh, mr(0, k), start=f, stop=False)
                        pe.matmul(mps, wh, mr(1, k), start=False, stop=False)
                        pe.matmul(mps, wl, mr(0, k), start=False, stop=l)
                    pe.matmul(ps, wh, ah, start=f, stop=False)
                    pe.matmul(ps, wh, al, start=False, stop=False)
                    mm = pe.matmul(ps, wl, ah, start=False, stop=l)
                    if (tau, 0) in PL.marks:
                        mm.then_inc(mm_done, 1)

            def out_N(s, lhs, meta=None):
                w = s.width * P
                for t in range(NQ):
                    bank_free(s.o0 + t)
                    ps = pS[:, (s.o0 + t) % 4, 0:w]
                    a = slice(t * P, (t + 1) * P)
                    for k in range(s.k):
                        tau = s.tile(0, k)
                        wh, wl = weights(tau, s.width)
                        f, l = k == 0, k == s.k - 1
                        if meta is not None and t == 0:
                            pe.matmul(meta, lhs(0, k)[:, T:TM], wh, start=f, stop=False)
                            pe.matmul(meta, lhs(0, k)[:, T:TM], wl, start=False, stop=False)
                            pe.matmul(meta, lhs(1, k)[:, T:TM], wh, start=False, stop=l)
                        pe.matmul(ps, lhs(0, k)[:, a], wh, start=f, stop=False)
                        pe.matmul(ps, lhs(0, k)[:, a], wl, start=False, stop=False)
                        mm = pe.matmul(ps, lhs(1, k)[:, a], wh, start=False, stop=l)
                        if (tau, t) in PL.marks:
                            mm.then_inc(mm_done, 1)

            def lead(s, name):
                r = PL.r[name]
                for k in range(s.k):
                    if k == s.k - 1:
                        norm_sum(name, name == "x0")
                    pe.wait_ge(rhs_ready, r + k + 1)
                    for j in range(LEAD):
                        o = s.o0 + j
                        if k == 0:
                            bank_free(o)
                        tau = s.tile(j, k)
                        wh, wl = weights(tau)
                        ps = pS[:, o % 4, :]
                        pe.matmul(ps, wh, xa[0][:, k, 0:T], start=k == 0, stop=False)
                        pe.matmul(ps, wl, xa[0][:, k, 0:T], start=False, stop=False)
                        mm = pe.matmul(ps, wh, xa[1][:, k, 0:T], start=False, stop=k == s.k - 1)
                        if (tau, 0) in PL.marks:
                            mm.then_inc(mm_done, 1)
                norm_spread(name, name == "x0")

            def norm_sum(name, meta=False):
                pe.wait_ge(sq_summed, PL.q[name] + dict(SQUARES)[name])
                if meta:
                    pe.matmul(pO[0:M, 1, 4:5], acc[:, T:TM], ones[:, 0:1], start=True, stop=True)
                for t in range(NQ):
                    mm = pe.matmul(pO[:, 1, t:t + 1], acc[:, t * P:(t + 1) * P], ones[:, 0:1], start=True, stop=True)
                mm.then_inc(norm_mm, 1)

            def norm_spread(name, meta=False):
                pe.wait_ge(diag_ready, NORM[name] + 1)
                if meta:
                    pe.matmul(pO[:, 1, 8:8 + M], ones[0:M, :], diag[0:M, T:TM], start=True, stop=True)
                pe.matmul(pT[:, 1, :], ones[:, :], diag[:, 0:T], start=True, stop=True).then_inc(norm_wide, 1)

            def norm(name, meta=False):
                norm_sum(name, meta)
                norm_spread(name, meta)

            def moved_pt(t):
                pe.wait_ge(pt_moved, t + 1)

            def product(out, l, r, start=True, stop=True):
                pe.matmul(out, l(0), r(0), start=start, stop=False)
                pe.matmul(out, l(0), r(1), start=False, stop=False)
                return pe.matmul(out, l(1), r(0), start=False, stop=stop)

            def item_free(i):
                if i < 2:
                    return
                kind, v = ITEMS[i - 2]
                if kind == "Y":
                    pe.wait_ge(rhs_ready, v + 1)
                else:
                    moved_pt(v)

            def score(ph, t):
                if t.t - ph.slots >= ph.t0:
                    pe.wait_ge(probs, t.t - ph.slots + 1)
                sl = (t.t % ph.slots) * (4 // ph.slots)
                qs = slice(t.qi * P, (t.qi + 1) * P)
                n = len(t.kb) * P
                k0 = t.kb[0] * P
                c0 = 384 - P * t.qi + k0
                if t.kind == "diff":
                    d = slice(t.s * HD, (t.s + 1) * HD)
                    product(pS[:, sl, :], lambda x: qa[x][d, t.h, qs], lambda x: ka[x][d, t.h, 0:T], stop=False)
                    pe.matmul(pS[:, sl, :], sident[:, 2 * t.h + 1, :], dist[:, c0:c0 + n], start=False, stop=True)
                    return
                elif t.kind == "win":
                    g = t.h // 4
                    d = slice(g * HD, (g + 1) * HD)
                    q = lambda x: qb[x][d, t.h % 4, qs]
                    product(pS[:, sl, n:n + M], q, lambda x: kb_[x][d, T:TM])
                    product(pS[:, sl, 0:n], q, lambda x: kb_[x][d, k0:k0 + n], stop=False)
                    pe.matmul(pS[:, sl, 0:n], sident[:, t.h, :], dist[:, c0:c0 + n], start=False, stop=False)
                    mm = pe.matmul(pS[:, sl, 0:n], identb[:, :], band[:, c0:c0 + n], start=False, stop=True)
                elif t.kind == "mla":
                    d = slice((t.h % 2) * HD, (t.h % 2 + 1) * HD)
                    r = slice((t.h % 4) * 32, (t.h % 4 + 1) * 32)
                    product(pS[:, sl, 0:n], lambda x: qn[x][d, t.h // 2, qs], lambda x: kn[x][d, t.h // 2, 0:n], stop=False)
                    product(pS[:, sl, 0:n], lambda x: qrp[x][r, t.h // 4, qs], lambda x: krp[x][r, 0:n], start=False,
                            stop=False)
                    mm = pe.matmul(pS[:, sl, n - P:n], identb[:, :], causal[:, :], start=False, stop=True)
                elif t.kind == "cmp":
                    for h in range(16):
                        g, r = h // 4, h % 4
                        mm = product(pS[:, sl, h * NCP:(h + 1) * NCP], lambda x: q2[x][:, (g // 2) * 4 + r, qs],
                                     lambda x: kct[x][:, g, :])
                else:
                    g, r = t.h // 4, t.h % 4
                    d = slice((g % 2) * HD, (g % 2 + 1) * HD)
                    k = (ks, kw)[t.b]
                    product(pS[:, sl, 0:n], lambda x: q2[x][d, (g // 2) * 4 + r, qs], lambda x: k[x][d, g // 2, 0:n],
                            stop=False)
                    pe.matmul(pS[:, sl, 0:n], aug[:, t.h, :], rel[:, c0:c0 + n], start=False, stop=False)
                    mm = pe.matmul(pS[:, sl, n - P:n], identb[:, :], causal[:, :], start=False, stop=True)
                mm.then_inc(scores, 1)

            def score_meta(ph, t):
                if t.t - ph.slots >= ph.t0:
                    moved_pt(t.t - ph.slots)
                d = slice(t.s * HD, (t.s + 1) * HD)
                qs = slice(t.qi * P, (t.qi + 1) * P)
                product(pS[:, (t.t % 2) * 2 + 1, 0:M], lambda x: qa[x][d, t.h, qs],
                        lambda x: ka[x][d, t.h, T:TM]).then_inc(scores, 1)

            def transpose_p(ph, t):
                pe.wait_ge(probs_split, t.t + 1)
                item_free(t.item)
                n = len(t.kb) * P
                for x in range(2):
                    p = p_hl[:, (t.t % 2) * 2 + x, :]
                    if t.kind in ("diff", "win"):
                        pe.transpose(meta_psum(t)[:, x, :], p[:, n:n + M], identh[:, :])
                    for b in range(len(t.kb)):
                        mm = pe.transpose(pt_psum(t.item)[:, x, b, :], p[:, b * P:(b + 1) * P], identh[:, :])
                mm.then_inc(transposed, 1)

            def attend(ph, t):
                moved_pt(t.t)
                G = ph.g0 + t.group
                if t.j == 0 and G >= 2:
                    pe.wait_ge(grp_out, G - 1)
                pt = pt_of(t.t)
                if t.kind == "cmp":
                    for g in range(4):
                        mm = product(pO[:, (G - 1 + g // 2) % 2, (g % 2) * 256:(g % 2 + 1) * 256],
                                     lambda x: pt[:, x, g, :], lambda x: vcbd[x][:, g, :])
                    mm.then_inc(av_done, 2)
                    return
                o = pO[:, G % 2, t.col:t.col + t.dv]
                nb = len(t.kb)
                if t.kind == "diff":
                    v, c = va, t.h * P
                elif t.kind == "win":
                    v, c = vb, (t.h // 4) * HD
                elif t.kind == "mla":
                    v, c = vm, t.h * HD
                else:
                    v, c = vv, t.b * 256 + (t.h // 4) * HD
                meta = t.kind in ("diff", "win")
                for b, k in enumerate(t.kb):
                    mm = product(o, lambda x: pt[:, x, b, :], lambda x: v[x][:, k, c:c + t.dv], start=b == 0,
                                 stop=b == nb - 1 and not meta)
                if meta:
                    mm = product(o, lambda x: pt[0:M, x, 4, :], lambda x: v[x][0:M, NQ, c:c + t.dv], start=False)
                if t.last:
                    mm.then_inc(av_done, 1)

            def transpose_y(ph, item, y):
                item_free(item)
                if ph.name == "diff":
                    pe.wait_ge(y_done, y + 1)
                elif ph.name == "nsa":
                    pe.wait_ge(pool_added, PH["diff"].n_groups + n_added(6 * (y // 2) + 4 + y % 2) + 1)
                else:
                    pe.wait_ge(grp_out, ph.g0 + y + 1)
                for b in range(2 if ph.name == "diff" else 4):
                    mm = pe.transpose(pT[:, item % 2, b * P:(b + 1) * P], o_nat[:, y % 4, b * P:(b + 1) * P], ident[:, :])
                mm.then_inc(transposed, 1)

            def attention(ph):
                ts = ph.tasks
                for t in ts[:ph.ahead]:
                    score(ph, t)
                    if t.kind == "diff":
                        score_meta(ph, t)
                for n, t in enumerate(ts):
                    transpose_p(ph, t)
                    nxt = ts[n + ph.ahead] if n + ph.ahead < len(ts) else None
                    if nxt is not None:
                        score(ph, nxt)
                    if n >= ph.lag:
                        attend(ph, ts[n - ph.lag])
                    if nxt is not None and t.kind == "diff":
                        score_meta(ph, nxt)
                    if n == len(ts) - 1:
                        for m in range(n - ph.lag + 1, n + 1):
                            attend(ph, ts[m])
                    for item, y in ph.y_at.get(n, []):
                        transpose_y(ph, item, y)
                pe.wait_ge(probs, ph.t1)

            def of(a):
                return lambda q, k: a[q][:, k, 0:T]

            xr = of(xa)
            xm = lambda q, k: xa[q][:, k, T:TM]
            full = lambda q, k: xa[q][:, k, :]
            pe.wait_ge(basics_ready, 1)
            lead(S["qa"], "x0")
            pe.wait_ge(rs_ready, 1)
            for j in range(4):
                out_T(S["ka"], j, xr, meta=(pT[:, 0, j * M:(j + 1) * M], xm))
            out_N(S["va"], full, meta=pT[0:M, 1, :])
            for j in range(4):
                out_T(S["qb"], j, xr)
            out_T(S["kb"], 0, xr, meta=(pO[:, 1, 0:M], xm))
            out_N(S["vb"], full, meta=pO[0:M, 0, 0:P])
            pe.wait_ge(tables_ready, 1)
            pe.wait_ge(rhs_ready, PL.r["vb"] + NQ)
            attention(PH["diff"])
            attention(PH["win"])
            for n in range(KD):
                out_T(S[f"mrg_ga{n}"], 0, xr)
                out_T(S[f"mrg_gb{n}"], 0, xr)
                if n == 0:
                    pe.wait_ge(rhs_ready, PL.r["mrg"])
                out_T(S[f"mrg_a{n}"], 0, of(ya_))
                out_T(S[f"mrg_b{n}"], 0, of(yb_))
            for j in range(KD):
                out_T(S["wo"], j, of(mg), rhs_wait=None if j else PL.r["mrg"])
            lead(S["ffgu"], "x1")
            for j in range(LEAD, 2 * KFF1):
                out_T(S["ffgu"], j, xr)
            for j in range(KD):
                out_T(S["ffd"], j, of(ffh), rhs_wait=None if j else PL.r["ff"])
            norm("x2")
            lead(S["cv"], "xb")
            for j in range(LEAD, 12):
                out_T(S["cv"], j, xr)
            for j in range(6):
                out_T(S["cq"], j, xr)
            out_T(S["ckv"], 0, xr)
            norm_sum("cq")
            out_T(S["ckv"], 1, xr)
            out_T(S["kr"], 0, xr)
            norm_spread("cq")

            def rope(n, o):
                pe.wait_ge(evicted, o + 1)
                if n:
                    pe.wait_ge(rope_done, n)
                pe.matmul(pT[:, 0, :], swap[:, :], qr[:, (2, 0, 1)[n], :], start=True, stop=True).then_inc(rope_mm, 1)

            pe.wait_ge(tables_ready, 1)
            for j in range(4):
                out_T(S["qn"], j, of(cqs), rhs_wait=None if j else PL.r["cq"])
            rope(0, S["kr"].o0)
            for j in range(2):
                out_T(S["qr"], j, of(cqs))
            out_T(S["kn"], 0, of(cks), rhs_wait=PL.r["ckv"])
            norm("ckv")
            for j in range(1, 4):
                out_T(S["kn"], j, of(cks))
            rope(1, S["qr"].o0)
            rope(2, S["qr"].o0 + 1)
            out_N(S["vm"], lambda q, k: cks[q][:, k, :])
            pe.wait_ge(rhs_ready, PL.r["vm"] + NQ)
            attention(PH["mla"])
            pe.wait_ge(rhs_ready, PL.r["p1"])
            for j in range(KD):
                out_T(S["awo"], j, of(mx))
            norm("ma")

            def mlp(lay, p_in, h, m):
                lead(S[f"up{lay}"], p_in)
                for j in range(LEAD, KFF2):
                    out_T(S[f"up{lay}"], j, xr)
                for j in range(KD):
                    out_T(S[f"dn{lay}"], j, of(ffh), rhs_wait=None if j else PL.r[h])
                norm(m)

            mlp(0, "p1", "h0", "mb")
            lead(S["kvc"], "p2")
            for j in range(2):
                out_T(S["ks"], j, xr)
            pe.wait_ge(rhs_ready, PL.r["ks"])
            for c, name in enumerate(("ck1", "cv1")):
                s = S[name]
                bank_free(s.o0)
                ps = pS[:, s.o0 % 4, 0:2 * NCMP].rearrange("p (a n) -> p a n", a=2)
                bs = pO[:, c, 0:1]
                for k in range(CL):
                    tau = s.tile(0, k)
                    wh, wl = weights(tau)
                    rh, rl = (z[q][:, 2 * c:2 * c + 2, k:k + 16 * (NCMP - 1) + 1:16] for q in range(2))
                    bh, bl = (pe_s[q][:, c * CL + k:c * CL + k + 1] for q in range(2))
                    f, l = k == 0, k == CL - 1
                    pe.matmul(bs, wh, bh, start=f, stop=False)
                    pe.matmul(bs, wh, bl, start=False, stop=False)
                    pe.matmul(bs, wl, bh, start=False, stop=l)
                    pe.matmul(ps, wh, rh, start=f, stop=False)
                    pe.matmul(ps, wh, rl, start=False, stop=False)
                    mm = pe.matmul(ps, wl, rh, start=False, stop=l)
                    if (tau, 0) in PL.marks:
                        mm.then_inc(mm_done, 1)
            for j in range(8):
                out_T(S["q2"], j, xr)
            for j in range(2):
                out_T(S["kw"], j, xr)
            out_N(S["vv"], full)
            out_T(S["ck2"], 0, lambda q, k: hid[q][:, 0, 0:2 * NCMP], n_cols=2 * NCMP, rhs_wait=PL.r["hid"])
            s = S["cv2"]
            bank_free(s.o0)
            pe.wait_ge(rhs_ready, PL.r["hid"] + 2)
            wh, wl = weights(s.tau0)
            for a in range(2):
                ps = pS[0:NCMP, s.o0 % 4, a * P:(a + 1) * P]
                hh, hl = (hid[q][:, 1, a * NCMP:(a + 1) * NCMP] for q in range(2))
                pe.matmul(ps, hh, wh, start=True, stop=False)
                pe.matmul(ps, hl, wh, start=False, stop=False)
                mm = pe.matmul(ps, hh, wl, start=False, stop=True)
            mm.then_inc(mm_done, 1)
            out_N(S["gt"], full)
            pe.wait_ge(evicted, S["gt"].o0 + NQ)
            attention(PH["nsa"])
            pe.wait_ge(rhs_ready, PL.r["p3"])
            for j in range(KD):
                out_T(S["cwo"], j, xr)
            norm("mc")
            mlp(1, "p3", "h1", "md")

        @block.scalar
        def _(act):
            n_hi = [0]

            def split_hi(tau_last, look=LOOK, most=WR):
                need, most = tau_last // TPU + 1, n_hi[0] + most
                while n_hi[0] < min(need + look, max(need, most), PL.n_units):
                    u = n_hi[0]
                    act.wait_ge(raw_loaded[u % RAW], 16 * (u // RAW + 1))
                    if u >= WR:
                        act.wait_ge(mm_done, PL.unit_ms[u - WR])
                    act.activation(w_hi[:, u % WR, :], w_raw[:, u % RAW, :], ACT.Copy, scale=WS).then_inc(hi_split, 1)
                    n_hi[0] += 1

            def out_of(s, j=0):
                split_hi(PL.out_tau[s.o0 + j], most=splits(s, j))

            def hi(r, dst, a, scale=1.0):
                act.activation(dst, a, ACT.Identity, scale=scale).then_inc(rhs_hi, 1)

            def hi_parts(name, dst):
                for n, (a, j) in enumerate(dst):
                    out_of(S[name], n)
                    act.wait_ge(evicted, S[name].o0 + n + 1)
                    hi(PL.r[name] + n, a[0][:, j, :], src[:, n % 2, 0:a[0].shape[2]])

            def square(q, a, n=T):
                if q >= 2:
                    act.wait_ge(sq_summed, q - 1)
                act.activation(sq[:, q % 2, 0:n], a, ACT.Square).then_inc(squared, 1)

            def norm_copy(name, after_mm=True, meta=False, to=None):
                act.wait_ge(norm_wide, NORM[name] + 1)
                f = 1.0 / WS if after_mm else 1.0
                to = rs if to is None else to
                if meta:
                    act.activation(to[:, T:TM], pO[:, 1, 8:8 + M], ACT.Copy, scale=f)
                act.activation(to[:, 0:T], pT[:, 1, :], ACT.Copy, scale=f).then_inc(rs_ready, 1)

            def probabilities(ph, t):
                act.wait_ge(maxed, t.t + 1)
                if t.t >= 2:
                    act.wait_ge(probs_split, t.t - 1)
                p = p_sb[:, t.t % 2, :]
                G = (ph.g0 + t.group) % 4
                if t.kind == "cmp":
                    act.activation(p[:, 0:T], p[:, 0:T], ACT.Exp).then_inc(probs, 1)
                    return
                s_ = score_view(ph, t)
                act.activation(p[:, 0:s_.shape[1]], s_, ACT.Exp, bias=nmax[:, G, t.j:t.j + 1],
                               accum_out=sums[:, G, t.j:t.j + 1]).then_inc(probs, 1)

            def move_pt(ph, t):
                act.wait_ge(transposed, t.item + 1)
                n = len(t.kb)
                if t.kind in ("diff", "win"):
                    act.activation(pt_of(t.t)[0:M, :, 4, :], meta_psum(t), ACT.Copy)
                act.activation(pt_of(t.t)[:, :, 0:n, :], pt_psum(t.item)[:, :, 0:n, :], ACT.Copy).then_inc(pt_moved, 1)

            def y_hi(ph, item, y, dst, scale):
                act.wait_ge(transposed, item + 1)
                d, s_ = y_parts(ph, y, dst[0], pT[:, item % 2, :])
                act.activation(d, s_, ACT.Identity, scale=scale).then_inc(rhs_hi, 1)

            def rows_square(g):
                act.wait_ge(pool_added, g + 1)
                for h in range(2):
                    a = tmp[:, 2 + g % 2, h * P:(h + 1) * P]
                    ins = act.activation(tmp[:, 2 + g % 2, (2 + h) * P:(3 + h) * P], a, ACT.Square,
                                         accum_out=ssq[:, g % 2, h:h + 1])
                ins.then_inc(rows_sq, 1)

            def sink(g):
                act.wait_ge(tanh_in, 1 + g + 1)
                act.activation(sink_e[:, :], sink_e[:, :], ACT.Exp).then_inc(sink_exp, 1)

            def attention(ph, y_dst, y_scale, look_tau):
                split_hi(look_tau)
                ts = ph.tasks
                for n in range(len(ts) + ph.lag):
                    if n < len(ts):
                        t = ts[n]
                        if t.kind == "win" and n and t.j == 0:
                            sink(t.group - 1)
                        probabilities(ph, t)
                    elif ph.name == "win" and n == len(ts):
                        sink(t.group)
                    for g in group_ends(ph, n - 5) if ph.name == "diff" and n < len(ts) else []:
                        rows_square(g)
                    if n >= ph.lag:
                        m = n - ph.lag
                        move_pt(ph, ts[m])
                        if ph.name == "diff" and m == len(ts) - 1:
                            rows_square(ph.n_groups - 2)
                            rows_square(ph.n_groups - 1)
                        for item, y in ph.y_at.get(m, []):
                            y_hi(ph, item, y, y_dst, y_scale)

            act.wait_ge(x_loaded, 16)
            act.wait_ge(par_loaded, 16)
            for k in range(KD):
                square(k, X[:, k, :], TM)
                hi(PL.r["x0"] + k, xa[0][:, k, :], X[:, k, :], pcol("g_mix", k))
                if k % 2:
                    split_hi(0, k // 2)
            act.wait_ge(basics_ready, 1)
            norm_copy("x0", meta=True)
            hi_parts("qa", [(qa, j) for j in range(4)])
            hi_parts("ka", [([x[:, :, 0:T] for x in ka], j) for j in range(4)])
            hi_parts("va", [(va, t) for t in range(NQ)])
            hi_parts("qb", [(qb, j) for j in range(4)])
            hi_parts("kb", [([x[:, 0:T].unsqueeze(1) for x in kb_], 0)])
            hi_parts("vb", [(vb, t) for t in range(NQ)])
            act.wait_ge(tanh_in, 1)
            act.activation(lam[:, 0:2], lam[:, 0:2], ACT.Exp).then_inc(act_out, 1)
            attention(PH["diff"], ya_, lam[:, 3:4], S["mrg_ga0"].tau0)
            attention(PH["win"], yb_, 1.0, S["mrg_ga0"].tau0)
            for n in range(KD):
                for c, name in enumerate(("ga", "gb")):
                    s = S[f"mrg_{name}{n}"]
                    out_of(s)
                    act.wait_ge(evicted, s.o0 + 1)
                    act.activation(tmp[:, c, :], tmp[:, c, :], ACT.Tanh, scale=0.5).then_inc(act_out, 1)
                out_of(S[f"mrg_a{n}"])
                out_of(S[f"mrg_b{n}"])
                act.wait_ge(computed, PL.s["mrg"] + n + 1)
                hi(PL.r["mrg"] + n, mg[0][:, n, :], src[:, n % 2, :], 0.5 / WS)
            for n in range(KD):
                out_of(S["wo"], n)
                act.wait_ge(evicted, S["wo"].o0 + n + 1)
                square(PL.q["x1"] + n, X[:, n, 0:T])
                hi(PL.r["x1"] + n, xa[0][:, n, 0:T], X[:, n, 0:T], pcol("g_ffn", n))
            norm_copy("x1")
            for n in range(KFF1):
                out_of(S["ffgu"], 2 * n)
                act.wait_ge(evicted, S["ffgu"].o0 + 2 * n + 1)
                act.activation(tmp[:, 1, :], tmp[:, 0, :], ACT.Tanh, scale=0.5).then_inc(act_out, 1)
                out_of(S["ffgu"], 2 * n + 1)
                act.wait_ge(computed, PL.s["ff"] + n + 1)
                hi(PL.r["ff"] + n, ffh[0][:, n, :], src[:, n % 2, :])
            for n in range(KD):
                out_of(S["ffd"], n)
                act.wait_ge(evicted, S["ffd"].o0 + n + 1)
                square(PL.q["x2"] + n, X[:, n, 0:T])
            norm_copy("x2", after_mm=False)
            for n in range(KD):
                act.wait_ge(computed, PL.s["xb"] + n + 1)
                hi(PL.r["xb"] + n, xa[0][:, n, 0:T], X[:, n, 0:T], pcol("g_pre0", n))
                square(PL.q["xb"] + n, X[:, n, 0:T])
            norm_copy("xb")
            for n in range(4):
                for j in range(3):
                    out_of(S["cv"], 3 * n + j)
                act.wait_ge(computed, PL.s["conv"] + n + 1)
                hi(PL.r["conv"] + n, mx[0][:, n, :], src[:, n % 2, :])
            for name, n_, dst in (("cq", 6, cqs), ("ckv", 2, cks)):
                for n in range(n_):
                    out_of(S[name], n)
                    act.wait_ge(evicted, S[name].o0 + n + 1)
                    square(PL.q[name] + n, src[:, n % 2, :])
                    hi(PL.r[name] + n, dst[0][:, n, :], src[:, n % 2, :], pcol("g_" + name, n))
            out_of(S["kr"], 0)
            norm_copy("cq", to=rsq)
            hi_parts("qn", [(qn, j) for j in range(4)])
            act.wait_ge(rope_done, 1)
            hi(PL.r["kr"], krp[0], qr[:, 2, :])
            for j in range(2):
                out_of(S["qr"], j)
            out_of(S["kn"], 0)
            act.wait_ge(evicted, S["kn"].o0)
            norm_copy("ckv", to=rsq)
            hi_parts("kn", [(kn, j) for j in range(4)])
            for j in range(2):
                act.wait_ge(rope_done, 2 + j)
                hi(PL.r["qr"] + j, qrp[0][:, j, :], qr[:, j, :])
            hi_parts("vm", [(vm, t) for t in range(NQ)])
            attention(PH["mla"], [mx[0][:, 4:8, :], mx[1][:, 4:8, :]], 1.0, S["awo"].tau0)

            def post_norm(s, m, g_in=None, p_name=None):
                for n in range(KD):
                    out_of(s, n)
                    act.wait_ge(evicted, s.o0 + n + 1)
                    square(PL.q[m] + n, m_view(m, n))
                norm_copy(m, after_mm=False)
                if p_name is None:
                    return
                for n in range(KD):
                    act.wait_ge(computed, PL.s[p_name] + n + 1)
                    hi(PL.r[p_name] + n, xa[0][:, n, 0:T], X[:, n, 0:T], pcol(g_in, n))
                    square(PL.q[p_name] + n, X[:, n, 0:T])

            def mlp(lay, p_in, h):
                norm_copy(p_in)
                for n in range(KFF2):
                    out_of(S[f"up{lay}"], n)
                    act.wait_ge(computed, PL.s[h] + n + 1)
                    hi(PL.r[h] + n, ffh[0][:, n, :], src[:, n % 2, :])

            post_norm(S["awo"], "ma", "g_mpre0", "p1")
            mlp(0, "p1", "h0")
            post_norm(S["dn0"], "mb", "g_pre1", "p2")
            norm_copy("p2")
            for j in range(4):
                out_of(S["kvc"], j)
                act.wait_ge(evicted, S["kvc"].o0 + j + 1)
                hi(PL.r["z"] + j, z[0][:, j, :], src[:, j % 2, :])
            hi(PL.r["pe"], pe_s[0], pcol("pe", 0, 64))
            hi_parts("ks", [(ks, j) for j in range(2)])
            for c, name in enumerate(("ck1", "cv1")):
                out_of(S[name], 0)
                act.wait_ge(tanh_in, 5 + c + 1)
                act.activation(tmp[:, 2, 0:2 * NCMP], tmp[:, 2, 0:2 * NCMP], ACT.Tanh,
                               scale=0.7978845608028654).then_inc(act_out, 1)
                act.wait_ge(computed, PL.s["hid"] + c + 1)
                hi(PL.r["hid"] + c, hid[0][:, c, 0:2 * NCMP], src[:, c, 0:2 * NCMP], 0.5)
            hi_parts("q2", [(q2, j) for j in range(8)])
            hi_parts("kw", [(kw, j) for j in range(2)])
            hi_parts("vv", [(vv, t) for t in range(NQ)])
            out_of(S["ck2"], 0)
            out_of(S["cv2"], 0)
            for j in range(NQ):
                out_of(S["gt"], j)
            act.wait_ge(evicted, S["gt"].o0 + NQ)
            gf = gates.rearrange("p a b -> p (a b)")
            act.activation(gf, gf, ACT.Tanh, scale=0.5).then_inc(act_out, 1)
            attention(PH["nsa"], xa, 1.0, S["cwo"].tau0)
            post_norm(S["cwo"], "mc", "g_mpre1", "p3")
            mlp(1, "p3", "h1")
            post_norm(S["dn1"], "md")

        @block.vector
        def _(dve):
            n_lo = [0]
            chain = [0]
            last_lo = [0]

            def formed(s, j):
                split_lo(PL.out_tau[s.o0 + j], look=0)
                dve.wait_ge(mm_done, PL.out_ms[s.o0 + j])


            def link(ins):
                chain[0] += 1
                return ins.then_inc(dve_chain, 1)

            def sync():
                dve.wait_ge(dve_chain, chain[0])

            def split_lo(tau_last, look=LOOK, most=WR):
                need, most = tau_last // TPU + 1, n_lo[0] + most
                while n_lo[0] < min(need + look, max(need, most), PL.n_units):
                    u = n_lo[0]
                    dve.wait_ge(hi_split, u + 1)
                    dve.scalar_tensor_tensor(out=w_lo[:, u % WR, :], in0=w_raw[:, u % RAW, :], scalar=WS,
                                             in1=w_hi[:, u % WR, :], op0=ALU.mult, op1=ALU.subtract).then_inc(lo_split, 1)
                    n_lo[0] += 1

            def out_of(s, j=0):
                o = s.o0 + j
                split_lo(PL.out_tau[o], most=splits(s, j))
                dve.wait_ge(mm_done, PL.out_ms[o])
                return pS[:, o % 4, :]

            def lo(r, dst, a, h, scale=1.0):
                last_lo[0] = r + 1
                dve.wait_ge(rhs_hi, r + 1)
                dve.scalar_tensor_tensor(out=dst, in0=a, scalar=scale, in1=h, op0=ALU.mult,
                                         op1=ALU.subtract).then_inc(rhs_ready, 1)

            def add_square(name, k, n=T):
                q = PL.q[name] + k
                dve.wait_ge(squared, q + 1)
                if k == 0:
                    dve.tensor_copy(acc[:, 0:n], sq[:, q % 2, 0:n]).then_inc(sq_summed, 1)
                else:
                    dve.wait_ge(sq_summed, q)
                    dve.tensor_tensor(acc[:, 0:n], acc[:, 0:n], sq[:, q % 2, 0:n], ALU.add).then_inc(sq_summed, 1)

            def norm_rstd(name, n=D, meta=False, to=None):
                dve.wait_ge(norm_mm, NORM[name] + 1)
                if meta:
                    link(dve.tensor_scalar(rt[0:M, 0, NQ:NQ + 1], pO[0:M, 1, 4:5], 1.0 / n, EPS, ALU.mult, ALU.add))
                dve.tensor_scalar(rt[:, 0, 0:NQ], pO[:, 1, 0:NQ], 1.0 / n, EPS, ALU.mult, ALU.add).then_inc(mean_ready, 1)
                dve.wait_ge(rstd_ready, NORM[name] + 1)
                for t in range(NQ):
                    ins = dve.tensor_scalar(diag[:, t * P:(t + 1) * P], ident[:, :], rt[:, 1, t:t + 1], None, ALU.mult)
                if meta:
                    ins = dve.tensor_scalar(diag[0:M, T:TM], ident[0:M, 0:M], rt[0:M, 1, NQ:NQ + 1], None, ALU.mult)
                ins.then_inc(diag_ready, 1)
                if meta:
                    link(dve.tensor_scalar(rn[0:M, NQ:NQ + 1], rt[0:M, 1, NQ:NQ + 1], 1.0 / WS, None, ALU.mult))
                if to is not None:
                    link(dve.tensor_scalar(to[:, 0:NQ], rt[:, 1, 0:NQ], 1.0 / WS, None, ALU.mult))

            def norm_done(name):
                dve.wait_ge(rs_ready, NORM[name] + 1)
                sync()

            def norm(name, **kw):
                norm_rstd(name, **kw)
                norm_done(name)

            def evict(s, j, dst, r=rs):
                ps = out_of(s, j)
                dve.tensor_tensor(dst, ps, r[:, 0:T], ALU.mult).then_inc(evicted, 1)

            def evict_scaled(s, j, dst, f, r=rs):
                ps = out_of(s, j)
                dve.scalar_tensor_tensor(out=dst, in0=ps, scalar=f, in1=r[:, 0:T], op0=ALU.mult,
                                         op1=ALU.mult).then_inc(evicted, 1)

            def evict_N(s, t, dst, w, rcol):
                ps = out_of(s, t)
                dve.tensor_scalar(dst, ps[:, 0:w], rcol, None, ALU.mult).then_inc(evicted, 1)

            def parts_of(name, dst, f=1.0, rcol=None, r=rs):
                s, r0 = S[name], PL.r[name]
                for n in range(len(dst) + 1):
                    if n < len(dst):
                        a, j = dst[n]
                        w = a[0].shape[2]
                        ps = out_of(s, n)
                        if last_lo[0]:
                            dve.wait_ge(rhs_ready, last_lo[0])
                        to = src[:, n % 2, 0:w]
                        if rcol is not None:
                            ins = dve.tensor_scalar(to, ps[:, 0:w], rcol[:, n:n + 1], None, ALU.mult)
                        elif f != 1.0:
                            ins = dve.scalar_tensor_tensor(out=to, in0=ps, scalar=f, in1=r[:, 0:T], op0=ALU.mult,
                                                           op1=ALU.mult)
                        else:
                            ins = dve.tensor_tensor(to, ps, r[:, 0:T], ALU.mult)
                        ins.then_inc(evicted, 1)
                    if n:
                        a, j = dst[n - 1]
                        w = a[0].shape[2]
                        moved(s, n - 1)
                        lo(r0 + n - 1, a[1][:, j, :], src[:, (n - 1) % 2, 0:w], a[0][:, j, :])

            def moved(s, j):
                dve.wait_ge(evicted, s.o0 + j + 1)

            def row_max(ph, t):
                dve.wait_ge(scores, t.t + 1)
                G = (ph.g0 + t.group) % 4
                s_ = score_view(ph, t)
                if t.kind == "cmp":
                    dve.wait_ge(probs_split, t.t - 1)
                    a = p_sb[:, t.t % 2, 0:T]
                    a3 = a.rearrange("p (h n) -> p h n", h=16)
                    link(dve.tensor_tensor(a, s_, cbias[:, t.qi, :], ALU.add))
                    sync()
                    link(dve.tensor_reduce(cst[:, 0, :], a3, AX.X, ALU.max))
                    sync()
                    dve.tensor_tensor(a3, a3, cst[:, 0, :].unsqueeze(2).broadcast_to([P, 16, NCP]),
                                      ALU.subtract).then_inc(maxed, 1)
                    return
                nm = nmax[:, G, t.j:t.j + 1]
                if t.kind == "win":
                    link(dve.tensor_reduce(nm, s_, AX.X, ALU.max, negate=True))
                    sync()
                    dve.tensor_tensor(nm, nm, nsink[:, t.h:t.h + 1], ALU.min).then_inc(maxed, 1)
                    if t.last:
                        dve.wait_ge(maxed, t.t + 1)
                        dve.tensor_tensor(sink_e[:, :], pcol("sink", 0, 8), nmax[:, G, :], ALU.add).then_inc(tanh_in, 1)
                else:
                    dve.tensor_reduce(nm, s_, AX.X, ALU.max, negate=True).then_inc(maxed, 1)

            def split_p(ph, t):
                dve.wait_ge(probs, t.t + 1)
                if t.kind == "cmp":
                    link(dve.tensor_reduce(cst[:, 1, :], p_sb[:, t.t % 2, 0:T].rearrange("p (h n) -> p h n", h=16),
                                           AX.X, ALU.add))
                if t.item >= 1 and t.t >= 2:
                    dve.wait_ge(transposed, items_done(t.t - 2))
                w = T if t.kind == "cmp" else len(t.kb) * P + (M if t.kind in ("diff", "win") else 0)
                p = p_sb[:, t.t % 2, 0:w]
                h, l = (p_hl[:, (t.t % 2) * 2 + x, 0:w] for x in range(2))
                link(dve.tensor_copy(h, p))
                sync()
                dve.tensor_tensor(l, p, h, ALU.subtract).then_inc(probs_split, 1)

            def bc(a, n, w):
                return a.unsqueeze(2).broadcast_to([P, n, w])

            def rows_free(ph, y):
                if y >= 4:
                    dve.wait_ge(transposed, y_item(ph, y - 4) + 1)

            def group_out(ph, g):
                G = ph.g0 + g
                b = pO[:, G % 2, :]
                s8 = sums[:, G % 4, :]
                c8 = scale8[:, G % 2, :]
                dve.wait_ge(av_done, G + 1)
                if ph.name == "diff":
                    link(dve.reciprocal(c8[:, 0:4], s8[:, 0:4]))
                    sync()
                    link(dve.tensor_tensor(c8[:, 0:4], c8[:, 0:4], sgn[:, :], ALU.mult))
                    sync()
                    if g >= 2:
                        dve.wait_ge(pool_added, g - 1)
                    dve.tensor_tensor(tmp[:, g % 2, :].rearrange("p (a e) -> p a e", a=4),
                                      b.rearrange("p (a e) -> p a e", a=4), bc(c8[:, 0:4], 4, P), ALU.mult).then_inc(grp_out, 1)
                    return
                b3 = b.rearrange("p (h e) -> p h e", h=8)
                if ph.name == "win":
                    dve.wait_ge(sink_exp, g + 1)
                    link(dve.tensor_tensor(s8, s8, sink_e[:, :], ALU.add))
                    sync()
                if ph.name in ("win", "mla"):
                    link(dve.reciprocal(c8, s8))
                    sync()
                    rows_free(ph, g)
                    dve.tensor_tensor(o_nat[:, g % 4, :].rearrange("p (h e) -> p h e", h=8), b3, bc(c8, 8, HD),
                                      ALU.mult).then_inc(grp_out, 1)
                    return
                qi, k = g // 6, g % 6
                half, br = k % 2, k // 2
                if br == 0:
                    link(dve.reciprocal(c8, cst[:, 1, half * 8:half * 8 + 8]))
                    sync()
                    link(dve.tensor_scalar(c8, c8, has[:, qi:qi + 1], None, ALU.mult))
                else:
                    link(dve.reciprocal(c8, s8))
                sync()
                link(dve.tensor_tensor(c8, c8, gates[:, qi, br * 16 + half * 8:br * 16 + half * 8 + 8], ALU.mult))
                sync()
                y = 2 * qi + half
                rows = o_nat[:, y % 4, :]
                if br == 0:
                    rows_free(ph, y)
                    dve.tensor_tensor(rows.rearrange("p (h e) -> p h e", h=8), b3, bc(c8, 8, HD), ALU.mult).then_inc(grp_out, 1)
                    return
                i = PH["diff"].n_groups + n_added(g)
                dve.wait_ge(pool_added, i - 1)
                dve.tensor_tensor(tmp[:, k % 2, :].rearrange("p (h e) -> p h e", h=8), b3, bc(c8, 8, HD),
                                  ALU.mult).then_inc(grp_out, 1)

            def y_lo(ph, item, y, dst, scale):
                dve.wait_ge(rhs_hi, ITEMS[item][1] + 1)
                d, s_ = y_parts(ph, y, dst[1], pT[:, item % 2, :])
                h, _ = y_parts(ph, y, dst[0], pT[:, item % 2, :])
                dve.scalar_tensor_tensor(out=d, in0=s_, scalar=scale, in1=h, op0=ALU.mult,
                                         op1=ALU.subtract).then_inc(rhs_ready, 1)

            def attention(ph, y_dst, y_scale, look_tau):
                split_lo(look_tau)
                ts = ph.tasks
                for t in ts[:ph.ahead]:
                    row_max(ph, t)
                for n in range(-1, len(ts)):
                    if n + 1 < len(ts):
                        split_p(ph, ts[n + 1])
                    if n < 0:
                        continue
                    for item, y in ph.y_at.get(n - 1, []):
                        y_lo(ph, item, y, y_dst, y_scale)
                    if n + ph.ahead < len(ts):
                        row_max(ph, ts[n + ph.ahead])
                    for g in group_ends(ph, n - ph.lag - 1):
                        group_out(ph, g)
                    if n == len(ts) - 1:
                        for m in range(n - ph.lag, n + 1):
                            for g in group_ends(ph, m):
                                group_out(ph, g)
                for item, y in ph.y_at.get(len(ts) - 1, []):
                    y_lo(ph, item, y, y_dst, y_scale)

            dve.memset(ones[:, :], 1.0)
            dve.memset(half_neg[:, :], -0.5).then_inc(basics_ready, 1)
            dve.wait_ge(par_loaded, 16)
            dve.wait_ge(x_loaded, 16)
            for k in range(KD):
                add_square("x0", k, TM)
                lo(PL.r["x0"] + k, xa[1][:, k, :], X[:, k, :], xa[0][:, k, :], pcol("g_mix", k))
                if k % 2:
                    split_lo(0, k // 2)
            dve.wait_ge(const_loaded, 16)
            link(dve.tensor_copy(ident[:, :], stage_c[:, CONST["ident"][0]:CONST["ident"][1]]))
            sync()
            norm("x0", meta=True, to=rn)
            parts_of("qa", [(qa, j) for j in range(4)], f=0.125)

            def table(name):
                a, b = CONST[name]
                return stage_c[:, a:b]

            dve.tensor_copy(swap[:, :], table("swap"))
            dve.tensor_copy(identb[:, :], table("ident"))
            dve.tensor_copy(identh[:, :], table("ident"))
            dve.tensor_copy(dist[:, :], table("dist"))
            dve.tensor_copy(band[:, :], table("band"))
            dve.tensor_copy(causal[:, :], table("causal"))
            dve.tensor_copy(aug[:, :, :].rearrange("p a b -> p (a b)"), table("aug"))
            dve.tensor_copy(rel[:, :], table("rel"))
            dve.tensor_copy(has[:, :], table("has"))
            for h in range(8):
                dve.tensor_scalar(sident[:, h, :], table("ident"), 2.0 ** -(h + 1), None, ALU.mult)
            link(dve.tensor_scalar(nsink[:, :], pcol("sink", 0, 8), -1.0, None, ALU.mult))
            dve.memset(sgn[:, :], 1.0).then_inc(tables_ready, 1)
            parts_of("ka", [([x[:, :, 0:T] for x in ka], j) for j in range(4)])
            mt = tmp[:, 3, :]

            def meta_parts(dst, a):
                link(dve.tensor_copy(dst[0], a))
                sync()
                link(dve.tensor_tensor(dst[1], a, dst[0], ALU.subtract))
                sync()

            for h in range(4):
                link(dve.tensor_tensor(mt[:, h * M:(h + 1) * M], pT[:, 0, h * M:(h + 1) * M], rs[:, T:TM], ALU.mult))
            sync()
            meta_parts([x[:, :, T:TM] for x in ka], mt[:, 0:4 * M].rearrange("p (a b) -> p a b", a=4))
            formed(S["va"], 0)
            link(dve.tensor_scalar(mt[0:M, :], pT[0:M, 1, :], rn[0:M, NQ:NQ + 1], None, ALU.mult))
            sync()
            meta_parts([x[0:M, NQ, :] for x in va], mt[0:M, :])
            parts_of("va", [(va, t) for t in range(NQ)], rcol=rn)
            parts_of("qb", [(qb, j) for j in range(4)], f=0.125)
            formed(S["kb"], 0)
            link(dve.tensor_tensor(mt[:, 0:M], pO[:, 1, 0:M], rs[:, T:TM], ALU.mult))
            sync()
            meta_parts([x[:, T:TM] for x in kb_], mt[:, 0:M])
            parts_of("kb", [([x[:, 0:T].unsqueeze(1) for x in kb_], 0)])
            formed(S["vb"], 0)
            link(dve.tensor_scalar(mt[0:M, 0:P], pO[0:M, 0, 0:P], rn[0:M, NQ:NQ + 1], None, ALU.mult))
            sync()
            meta_parts([x[0:M, NQ, :] for x in vb], mt[0:M, 0:P])
            parts_of("vb", [(vb, t) for t in range(NQ)], rcol=rn)
            lq = pcol("lam", 0, 256).rearrange("p (a b d) -> p a b d", a=2, b=2)
            t0 = tmp[:, 0, 0:P].rearrange("p (a d) -> p a d", a=2)
            link(dve.tensor_tensor(t0, lq[:, :, 0, :], lq[:, :, 1, :], ALU.mult))
            sync()
            dve.tensor_reduce(lam[:, 0:2], t0, AX.X, ALU.add).then_inc(tanh_in, 1)
            dve.wait_ge(act_out, 1)
            link(dve.tensor_tensor(lam[:, 2:3], lam[:, 1:2], lam[:, 0:1], ALU.subtract))
            link(dve.tensor_scalar(lam[:, 3:4], pcol("g_sub"), 1.0 - LINIT, None, ALU.mult))
            sync()
            for c in (1, 3):
                link(dve.tensor_scalar(sgn[:, c:c + 1], lam[:, 2:3], -LINIT, None, ALU.add))
            sync()
            attention(PH["diff"], ya_, lam[:, 3:4], S["mrg_ga0"].tau0)
            attention(PH["win"], yb_, 1.0, S["mrg_ga0"].tau0)
            for n in range(KD):
                for c, name in enumerate(("ga", "gb")):
                    evict(S[f"mrg_{name}{n}"], 0, tmp[:, c, :])
                for c, name in enumerate(("a", "b")):
                    s = S[f"mrg_{name}{n}"]
                    ps = out_of(s)
                    dve.wait_ge(act_out, 1 + 2 * n + c + 1)
                    dve.scalar_tensor_tensor(out=tmp[:, 2 + c, :], in0=tmp[:, c, :], scalar=1.0, in1=ps, op0=ALU.add,
                                             op1=ALU.mult).then_inc(evicted, 1)
                moved(s, 0)
                dve.tensor_tensor(src[:, n % 2, :], tmp[:, 2, :], tmp[:, 3, :], ALU.add).then_inc(computed, 1)
                lo(PL.r["mrg"] + n, mg[1][:, n, :], src[:, n % 2, :], mg[0][:, n, :], 0.5 / WS)

            def residual(s, n, f):
                ps = out_of(s, n)
                dve.scalar_tensor_tensor(out=X[:, n, 0:T], in0=ps, scalar=f, in1=X[:, n, 0:T], op0=ALU.mult,
                                         op1=ALU.add).then_inc(evicted, 1)

            for n in range(KD + 1):
                if n < KD:
                    residual(S["wo"], n, 1.0 / WS)
                if n:
                    add_square("x1", n - 1)
                    lo(PL.r["x1"] + n - 1, xa[1][:, n - 1, 0:T], X[:, n - 1, 0:T], xa[0][:, n - 1, 0:T], pcol("g_ffn", n - 1))
            norm("x1")
            s = S["ffgu"]
            for n in range(KFF1):
                evict(s, 2 * n, tmp[:, 0, :])
                evict(s, 2 * n + 1, tmp[:, 2, :])
                dve.wait_ge(act_out, 17 + n + 1)
                link(dve.scalar_tensor_tensor(out=tmp[:, 3, :], in0=tmp[:, 1, :], scalar=1.0, in1=tmp[:, 0, :],
                                              op0=ALU.add, op1=ALU.mult))
                sync()
                dve.tensor_tensor(src[:, n % 2, :], tmp[:, 3, :], tmp[:, 2, :], ALU.mult).then_inc(computed, 1)
                lo(PL.r["ff"] + n, ffh[1][:, n, :], src[:, n % 2, :], ffh[0][:, n, :])
            for n in range(KD + 1):
                if n < KD:
                    residual(S["ffd"], n, 0.5 / WS)
                if n:
                    add_square("x2", n - 1)
            norm("x2")
            for n in range(KD + 1):
                if n < KD:
                    dve.scalar_tensor_tensor(out=X[:, n, 0:T], in0=X[:, n, 0:T], scalar=pcol("g_fin", n),
                                             in1=rs[:, 0:T], op0=ALU.mult, op1=ALU.mult).then_inc(computed, 1)
                if n:
                    lo(PL.r["xb"] + n - 1, xa[1][:, n - 1, 0:T], X[:, n - 1, 0:T], xa[0][:, n - 1, 0:T], pcol("g_pre0", n - 1))
                    add_square("xb", n - 1)
            norm("xb")
            link(dve.memset(vpad[:, 0:2], 0.0))
            s = S["cv"]
            for n in range(4):
                evict(s, 3 * n, tmp[:, 0, :])
                evict(s, 3 * n + 1, tmp[:, 1, :])
                moved(s, 3 * n + 1)
                link(dve.tensor_tensor(vpad[:, 2:2 + T], tmp[:, 0, :], tmp[:, 1, :], ALU.mult))
                sync()
                link(dve.tensor_scalar(tmp[:, 2, :], vpad[:, 2:2 + T], pcol("conv", 3 * n + 2), None, ALU.mult))
                for c in (1, 0):
                    sync()
                    link(dve.scalar_tensor_tensor(out=tmp[:, 2, :], in0=vpad[:, c:c + T], scalar=pcol("conv", 3 * n + c),
                                                  in1=tmp[:, 2, :], op0=ALU.mult, op1=ALU.add))
                evict(s, 3 * n + 2, tmp[:, 0, :])
                sync()
                moved(s, 3 * n + 2)
                dve.tensor_tensor(src[:, n % 2, :], tmp[:, 2, :], tmp[:, 0, :], ALU.mult).then_inc(computed, 1)
                lo(PL.r["conv"] + n, mx[1][:, n, :], src[:, n % 2, :], mx[0][:, n, :])
            for name, n_, dst in (("cq", 6, cqs), ("ckv", 2, cks)):
                for n in range(n_):
                    evict(S[name], n, src[:, n % 2, :])
                    if name == "ckv" and n == 0:
                        dve.wait_ge(norm_mm, NORM["cq"] + 1)
                    add_square(name, n)
                    lo(PL.r[name] + n, dst[1][:, n, :], src[:, n % 2, :], dst[0][:, n, :], pcol("g_" + name, n))
                    if name == "ckv" and n == 0:
                        norm_rstd("cq", n=768)
            evict(S["kr"], 0, qr[:, 2, :])
            norm_done("cq")

            def rope(n):
                if n == 0:
                    dve.wait_ge(table_loaded, 32)
                a = qr[:, (2, 0, 1)[n], :]
                dve.wait_ge(rope_mm, n + 1)
                link(dve.tensor_tensor(tmp[:, 0, :], a, cos, ALU.mult))
                link(dve.tensor_tensor(tmp[:, 1, :], pT[:, 0, :], sin, ALU.mult))
                sync()
                dve.tensor_tensor(a, tmp[:, 0, :], tmp[:, 1, :], ALU.add).then_inc(rope_done, 1)

            parts_of("qn", [(qn, j) for j in range(4)], MLA_SCALE, r=rsq)
            rope(0)
            lo(PL.r["kr"], krp[1], qr[:, 2, :], krp[0])
            for j in range(2):
                evict_scaled(S["qr"], j, qr[:, j, :], MLA_SCALE, rsq)
            norm("ckv", n=256, to=rnk)
            parts_of("kn", [(kn, j) for j in range(4)], r=rsq)
            rope(1)
            rope(2)
            for j in range(2):
                lo(PL.r["qr"] + j, qrp[1][:, j, :], qr[:, j, :], qrp[0][:, j, :])
            parts_of("vm", [(vm, t) for t in range(NQ)], rcol=rnk)
            attention(PH["mla"], [mx[0][:, 4:8, :], mx[1][:, 4:8, :]], 1.0, S["awo"].tau0)

            def post_norm(s, m, g_post, next_, g_in=None):
                for n in range(KD + 1):
                    if n < KD:
                        ps = out_of(s, n)
                        dve.tensor_scalar(m_view(m, n), ps, 1.0 / WS, None, ALU.mult).then_inc(evicted, 1)
                    if n:
                        add_square(m, n - 1)
                norm(m)
                for n in range(KD + 1):
                    if n < KD:
                        link(dve.scalar_tensor_tensor(out=tmp[:, n % 2, :], in0=m_view(m, n), scalar=pcol(g_post, n),
                                                      in1=rs[:, 0:T], op0=ALU.mult, op1=ALU.mult))
                        sync()
                        dve.tensor_tensor(X[:, n, 0:T], X[:, n, 0:T], tmp[:, n % 2, :], ALU.add).then_inc(computed, 1)
                    if n and g_in is not None:
                        lo(PL.r[next_] + n - 1, xa[1][:, n - 1, 0:T], X[:, n - 1, 0:T], xa[0][:, n - 1, 0:T], pcol(g_in, n - 1))
                        add_square(next_, n - 1)

            def mlp(lay, p_in, h, m):
                norm(p_in)
                s = S[f"up{lay}"]
                for n in range(KFF2 + 1):
                    if n < KFF2:
                        evict(s, n, tmp[:, n % 2, :])
                        moved(s, n)
                        dve.scalar_tensor_tensor(out=src[:, n % 2, :], in0=tmp[:, n % 2, :], scalar=0.0,
                                                 in1=tmp[:, n % 2, :], op0=ALU.max, op1=ALU.mult).then_inc(computed, 1)
                    if n:
                        lo(PL.r[h] + n - 1, ffh[1][:, n - 1, :], src[:, (n - 1) % 2, :], ffh[0][:, n - 1, :])

            post_norm(S["awo"], "ma", "g_post0", "p1", "g_mpre0")
            mlp(0, "p1", "h0", "mb")
            post_norm(S["dn0"], "mb", "g_mpost0", "p2", "g_pre1")
            norm("p2", to=rn)
            for j in range(4):
                evict(S["kvc"], j, src[:, j % 2, :])
                lo(PL.r["z"] + j, z[1][:, j, :], src[:, j % 2, :], z[0][:, j, :])
            lo(PL.r["pe"], pe_s[1], pcol("pe", 0, 64), pe_s[0])
            parts_of("ks", [(ks, j) for j in range(2)])
            for a in kct + vcbd:
                link(dve.memset(a, 0.0))
            nc2 = 2 * NCMP
            for c, name in enumerate(("ck1", "cv1")):
                ps = out_of(S[name], 0)
                link(dve.tensor_scalar(cst[:, 2, c:c + 1], pO[:, c, 0:1], 1.0 / WS, None, ALU.mult))
                sync()
                dve.tensor_scalar(tmp[:, 0, 0:nc2], ps[:, 0:nc2], 1.0 / WS, cst[:, 2, c:c + 1], ALU.mult,
                                  ALU.add).then_inc(evicted, 1)
                moved(S[name], 0)
                zz = tmp[:, 0, 0:nc2]
                t1 = tmp[:, 1, 0:nc2]
                link(dve.tensor_tensor(t1, zz, zz, ALU.mult))
                sync()
                link(dve.tensor_scalar(t1, t1, 0.044715, 1.0, ALU.mult, ALU.add))
                sync()
                dve.tensor_tensor(tmp[:, 2, 0:nc2], t1, zz, ALU.mult).then_inc(tanh_in, 1)
                dve.wait_ge(act_out, 40 + c)
                dve.scalar_tensor_tensor(out=src[:, c, 0:nc2], in0=tmp[:, 2, 0:nc2], scalar=1.0, in1=zz, op0=ALU.add,
                                         op1=ALU.mult).then_inc(computed, 1)
                lo(PL.r["hid"] + c, hid[1][:, c, 0:nc2], src[:, c, 0:nc2], hid[0][:, c, 0:nc2], 0.5)
            parts_of("q2", [(q2, j) for j in range(8)], 0.125)
            parts_of("kw", [(kw, j) for j in range(2)])
            parts_of("vv", [(vv, t) for t in range(NQ)], rcol=rn)
            ps = out_of(S["ck2"], 0)
            link(dve.tensor_scalar(tmp[:, 0, 0:nc2], ps[:, 0:nc2], 1.0 / WS, None, ALU.mult))
            sync()
            for x in range(2):
                for g in range(4):
                    d = slice((g % 2) * HD, (g % 2 + 1) * HD)
                    a = tmp[d, 0, (g // 2) * NCMP:(g // 2 + 1) * NCMP]
                    if x == 0:
                        ins = link(dve.tensor_copy(kct[0][d, g, 0:NCMP], a))
                    else:
                        ins = dve.tensor_tensor(kct[1][d, g, 0:NCMP], a, kct[0][d, g, 0:NCMP], ALU.subtract)
                if x == 0:
                    sync()
            ins.then_inc(evicted, 1)
            ps = out_of(S["cv2"], 0)
            for r in range(4):
                rows, cols = slice(r * NCP, r * NCP + NCMP), slice(r * HD, (r + 1) * HD)
                a = tmp[rows, 1, 0:256].rearrange("p (g d) -> p g d", g=4)
                link(dve.tensor_scalar(tmp[rows, 1, 0:256], ps[0:NCMP, 0:256], 1.0 / WS, None, ALU.mult))
                sync()
                link(dve.tensor_copy(vcbd[0][rows, :, cols], a))
                sync()
                ins = dve.tensor_tensor(vcbd[1][rows, :, cols], a, vcbd[0][rows, :, cols], ALU.subtract)
                if r < 3:
                    link(ins)
            ins.then_inc(evicted, 1)
            for t in range(NQ):
                evict_N(S["gt"], t, gates[:, t, :], 48, rn[:, t:t + 1])
            dve.wait_ge(act_out, 42)
            gf = gates.rearrange("p a b -> p (a b)")
            link(dve.tensor_scalar(gf, gf, 0.5, 0.5, ALU.mult, ALU.add))
            sync()
            dve.wait_ge(table_loaded, 48)
            attention(PH["nsa"], xa, 1.0, S["cwo"].tau0)
            post_norm(S["cwo"], "mc", "g_post1", "p3", "g_mpre1")
            mlp(1, "p3", "h1", "md")
            post_norm(S["dn1"], "md", "g_mpost1", "out")

        @block.sync
        def _(sp):
            sp.dma_start(par[:, :], params).then_inc(par_loaded, 16)
            sp.dma_start(X[:, :, :], x_in).then_inc(x_loaded, 16)
            for u in range(RAW):
                sp.dma_start(w_raw[:, u, :], stream[u]).then_inc(raw_loaded[u], 16)
            sp.dma_start(stage_c, consts[:, 0:KEEP_TO]).then_inc(const_loaded, 16)

            def units(lo, hi):
                rounds = (hi - lo) // RAW
                if rounds > 1:
                    with sp.Fori(0, rounds) as i:
                        for u in range(lo, lo + RAW):
                            sp.wait_ge(lo_split, i * RAW + (u - RAW + 1))
                            sp.dma_start(w_raw[:, u % RAW, :], stream[bass.ds(i * RAW + u, 1), :, :].rearrange("o p w -> (o p) w")).then_inc(raw_loaded[u % RAW], 16)
                    lo += rounds * RAW
                for u in range(lo, hi):
                    sp.wait_ge(lo_split, u - RAW + 1)
                    sp.dma_start(w_raw[:, u % RAW, :], stream[u]).then_inc(raw_loaded[u % RAW], 16)

            u1 = S["kr"].tau0 // TPU
            units(RAW, u1)
            sp.wait_ge(mm_done, PL.out_ms[S["cv"].o0 - 1])
            for name, v in (("cos", cos), ("sin", sin)):
                a, b = CONST[name]
                sp.dma_start(v, consts[:, a:b]).then_inc(table_loaded, 16)
            u2 = S["q2"].tau0 // TPU
            units(u1, u2)
            sp.wait_ge(mm_done, PL.out_ms[S["kvc"].o0 - 1])
            a, b = CONST["cmpbias"]
            sp.dma_start(cbias.rearrange("p a b -> p (a b)"), consts[:, a:b]).then_inc(table_loaded, 16)
            units(u2, PL.n_units)
            for k in range(KD):
                sp.wait_ge(computed, PL.s["out"] + k + 1)
                sp.dma_start(out[:, k, :], X[:, k, 0:T]).then_inc(out_stored, 16)
            sp.wait_ge(out_stored, 16 * KD)

    return nc


def pack_stream(i):
    s = {}
    wi = i["w_in"][0]
    c = np.cumsum([0, 512, 512, 512, 512, 128, 128, 1024, 1024])
    s["qa"], s["ka"], s["va"], qb, s["kb"], s["vb"], ga, gb = (wi[:, c[n]:c[n + 1]] for n in range(8))
    s["qb"] = qb.reshape(D, 2, 4, HD).transpose(0, 2, 1, 3).reshape(D, 512)
    for n in range(KD):
        cols = slice(n * P, (n + 1) * P)
        s[f"mrg_ga{n}"], s[f"mrg_gb{n}"] = ga[:, cols], gb[:, cols]
        s[f"mrg_a{n}"], s[f"mrg_b{n}"] = i["w_branch_a"][0][:, cols], i["w_branch_b"][0][:, cols]
    s["wo"] = i["w_out"][0]
    s["ffgu"] = np.stack([i["w_ff_gate"][0].reshape(D, KFF1, P), i["w_ff_up"][0].reshape(D, KFF1, P)], 2).reshape(D, -1)
    s["ffd"] = i["w_ff_down"][0]
    a = i["a_w_in_2"][0]
    gb_, gc_, hv = (a[:, n * 512:(n + 1) * 512].reshape(D, 4, P) for n in range(3))
    s["cv"] = np.stack([gc_, hv, gb_], 2).reshape(D, -1)
    s["cq"], s["ckv"] = a[:, 1536:2304], a[:, 2304:2560]
    s["kr"] = np.tile(a[:, 2560:2592], (1, 4))
    q = i["a_w_q_up_2"][0].reshape(768, 8, 96)
    s["qn"], s["qr"] = q[:, :, :64].reshape(768, 512), q[:, :, 64:].reshape(768, 256)
    kv = i["a_w_kv_up_2"][0].reshape(256, 8, P)
    s["kn"], s["vm"] = kv[:, :, :64].reshape(256, 512), kv[:, :, 64:].reshape(256, 512)
    s["awo"] = i["a_w_out_2"][0]
    cw = i["c_w_in_2"][0]
    s["q2"] = cw[:, :1024].reshape(D, 2, 2, 4, HD).transpose(0, 1, 3, 2, 4).reshape(D, 1024)
    kc, vc, ks, vs, kw, vw = (cw[:, 1024 + 256 * n:1280 + 256 * n] for n in range(6))
    s["kvc"], s["ks"], s["kw"] = np.concatenate([kc, vc], 1), ks, kw
    s["vv"] = np.concatenate([vs, vw], 1)
    s["gt"] = np.concatenate([cw[:, 2560:], np.zeros((D, 80), np.float32)], 1)

    def twice(w):
        b = np.zeros(w.shape[:-2] + (P, P), np.float32)
        b[..., :64, :64] = w
        b[..., 64:, 64:] = w
        return b.reshape(-1, P)

    s["ck1"], s["cv1"] = twice(i["c_cmp_w1_k_2"][0]), twice(i["c_cmp_w1_v_2"][0])
    s["ck2"], s["cv2"] = twice(i["c_cmp_w2_k_2"][0]), twice(i["c_cmp_w2_v_2"][0])
    s["cwo"] = i["c_w_out_2"][0]
    for lay in range(2):
        s[f"up{lay}"], s[f"dn{lay}"] = i["mlp_w1_2"][lay], i["mlp_w2_2"][lay]
    tiles = np.zeros((PL.n_units * TPU, P, P), np.float32)
    for st in PL.order:
        n = st.n if st.kind == "T" else st.width
        w = s[st.name].reshape(st.k, P, n, P)
        if st.name in LEADS:
            lead = w[:, :, :LEAD].transpose(0, 2, 1, 3).reshape(-1, P, P)
            w = np.concatenate([lead, w[:, :, LEAD:].transpose(2, 0, 1, 3).reshape(-1, P, P)], 0)
        else:
            w = w.transpose(2, 0, 1, 3) if st.kind == "T" else w.transpose(0, 2, 1, 3)
        tiles[st.tau0:st.tau0 + n * st.k] = w.reshape(-1, P, P)
    return np.ascontiguousarray(tiles.reshape(PL.n_units, TPU, P, P).transpose(0, 2, 1, 3)).reshape(PL.n_units, P, UW)


def pack_params(i):
    def cols(g):
        return np.asarray(g, np.float32).reshape(-1, P).T

    def rows(g):
        return np.broadcast_to(np.asarray(g, np.float32).reshape(1, -1), (P, np.size(g)))

    def dup(pe):
        return np.concatenate([pe.T, pe.T], 0)

    parts = {"g_mix": cols(i["norm_mix"]), "g_ffn": cols(i["norm_ffn"]), "g_fin": cols(i["norm_final"]),
             "g_sub": cols(i["subln_gain"]), "g_cq": cols(i["a_q_norm_2"]), "g_ckv": cols(i["a_kv_norm_2"]),
             "conv": i["a_conv_w_2"][0].reshape(3, 4, P).transpose(2, 1, 0).reshape(P, 12),
             "sink": rows(i["sink_logits"]),
             "lam": rows(np.concatenate([i["lambda_q1"], i["lambda_k1"], i["lambda_q2"], i["lambda_k2"]], 0)),
             "pe": np.concatenate([dup(i["c_cmp_pe_k_2"][0]), dup(i["c_cmp_pe_v_2"][0])], 1)}
    for lay in range(2):
        parts[f"g_pre{lay}"], parts[f"g_post{lay}"] = cols(i["norm_mix_pre_2"][lay]), cols(i["norm_mix_post_2"][lay])
        parts[f"g_mpre{lay}"], parts[f"g_mpost{lay}"] = cols(i["norm_mlp_pre_2"][lay]), cols(i["norm_mlp_post_2"][lay])
    return np.ascontiguousarray(np.concatenate([parts[n] for n in PARAM], 1))


def kernel(**inputs):
    from concourse import bacc
    from concourse.bass_utils import run_bass_kernel_spmd

    i = {k: np.asarray(v) for k, v in inputs.items()}
    xt = np.concatenate([i["x"][0], i["meta_tokens"]], 0).T.reshape(KD, P, TM).transpose(1, 0, 2)
    arrays = {"in_x": np.ascontiguousarray(xt), "in_w": pack_stream(i), "in_c": CONSTANTS, "in_p": pack_params(i)}
    nc = bacc.Bacc("TRN2", target_bir_lowering=False, num_devices=1)
    args = [nc.dram_tensor(n, a.shape, F32, kind="ExternalInput").ap() for n, a in arrays.items()]
    args.append(nc.dram_tensor("out_t", (P, KD, T), F32, kind="ExternalOutput").ap())
    build_program(nc, *args)
    r = run_bass_kernel_spmd(nc, [arrays], core_ids=[0])
    y = r.results[0]["out_t"]
    return np.ascontiguousarray(y.transpose(2, 1, 0).reshape(1, T, D))
```
